# Optimizing a Trainium2 kernel written in Bass

```python
import math
import jax, jax.numpy as jnp
from jax import lax
import numpy as np

D_MODEL = 1024
BATCH = 1
SEQ = 1024
DEPTH = 1

N_Q_HEADS = 8
N_KV_HEADS = 2
HEAD_DIM = 64
Q_GROUP = N_Q_HEADS // N_KV_HEADS
ATTN_WIDTH = N_Q_HEADS * HEAD_DIM
KV_WIDTH = N_KV_HEADS * HEAD_DIM
WINDOW = 128
BLOCK = 128
N_BUCKETS = 32
MAX_DISTANCE = 128
NEG_INF = -1e30
SSM_WIDTH = D_MODEL // 2
SSM_GROUP = 16
SSM_GROUPS = SSM_WIDTH // SSM_GROUP
SSM_STATE = 64
DT_MIN = 1e-3
DT_MAX = 1e-1
N_BRANCHES = 2
D_FF = 4 * D_MODEL
IN_WIDTH = ATTN_WIDTH + 2 * KV_WIDTH + SSM_WIDTH + N_BRANCHES * D_MODEL
SPLITS = (ATTN_WIDTH, ATTN_WIDTH + KV_WIDTH, ATTN_WIDTH + 2 * KV_WIDTH,
          ATTN_WIDTH + 2 * KV_WIDTH + SSM_WIDTH, ATTN_WIDTH + 2 * KV_WIDTH + SSM_WIDTH + D_MODEL)
RMS_EPS = 1e-6


def rmsnorm(x, g):
    xf = x.astype(jnp.float32)
    y = xf * lax.rsqrt(jnp.mean(xf * xf, axis=-1, keepdims=True) + RMS_EPS)
    return (y * g.astype(jnp.float32)).astype(x.dtype)

def t5_causal_bucket(dist):
    max_exact = N_BUCKETS // 2
    d = jnp.maximum(dist, 0)
    df = jnp.maximum(d, 1).astype(jnp.float32)
    large = max_exact + (jnp.log(df / max_exact) / math.log(MAX_DISTANCE / max_exact)
                         * (N_BUCKETS - max_exact)).astype(jnp.int32)
    large = jnp.minimum(large, N_BUCKETS - 1)
    return jnp.where(d < max_exact, d, large)

def sliding_window_attention(q, k, v, sinks, rel_bias):
    B, L = q.shape[0], q.shape[1]
    nb = L // BLOCK
    qb = q.reshape(B, nb, BLOCK, N_KV_HEADS, Q_GROUP, HEAD_DIM)

    def band(t):
        tb = t.reshape(B, nb, BLOCK, N_KV_HEADS, HEAD_DIM)
        prev = jnp.pad(tb, ((0, 0), (1, 0), (0, 0), (0, 0), (0, 0)))[:, :-1]
        return jnp.concatenate([prev, tb], axis=2)

    kb, vb = band(k), band(v)
    logits = jnp.einsum('bnqkgd,bnskd->bnkgqs', qb, kb,
                        preferred_element_type=jnp.float32) * (HEAD_DIM ** -0.5)
    qi = jnp.arange(BLOCK)[:, None]
    kj = jnp.arange(2 * BLOCK)[None, :]
    dist = qi + BLOCK - kj
    band_ok = (dist >= 0) & (dist < WINDOW)
    key_pos = jnp.arange(nb)[:, None] * BLOCK - BLOCK + jnp.arange(2 * BLOCK)[None, :]
    mask = band_ok[None] & (key_pos >= 0)[:, None, :]
    bias = rel_bias.astype(jnp.float32)[t5_causal_bucket(dist)]
    bias = jnp.transpose(bias, (2, 0, 1)).reshape(N_KV_HEADS, Q_GROUP, BLOCK, 2 * BLOCK)
    logits = jnp.where(mask[None, :, None, None], logits + bias[None, None], NEG_INF)
    s = sinks.astype(jnp.float32).reshape(1, 1, N_KV_HEADS, Q_GROUP, 1, 1)
    m = jnp.maximum(jnp.max(logits, axis=-1, keepdims=True), s)
    p = jnp.exp(logits - m)
    denom = jnp.sum(p, axis=-1, keepdims=True) + jnp.exp(s - m)
    probs = (p / denom).astype(v.dtype)
    out = jnp.einsum('bnkgqs,bnskd->bnqkgd', probs, vb)
    return out.reshape(B, L, ATTN_WIDTH)

def s5_ssm(u, lam_re, lam_im, log_dt, b_re, b_im, c_re, c_im, d_skip):
    B, L = u.shape[0], u.shape[1]
    uf = u.astype(jnp.float32).reshape(B, L, SSM_GROUPS, SSM_GROUP)
    dt = jnp.exp(log_dt.astype(jnp.float32))[:, None]
    lr = lam_re.astype(jnp.float32)
    li = lam_im.astype(jnp.float32)
    mag = jnp.exp(lr * dt)
    ab_re = mag * jnp.cos(li * dt)
    ab_im = mag * jnp.sin(li * dt)
    nr = ab_re - 1.0
    den = lr * lr + li * li
    f_re = (nr * lr + ab_im * li) / den
    f_im = (ab_im * lr - nr * li) / den
    br = b_re.astype(jnp.float32)
    bi = b_im.astype(jnp.float32)
    bb_re = f_re[..., None] * br - f_im[..., None] * bi
    bb_im = f_re[..., None] * bi + f_im[..., None] * br
    bu_re = jnp.einsum('blgc,gpc->blgp', uf, bb_re)
    bu_im = jnp.einsum('blgc,gpc->blgp', uf, bb_im)
    a_re = jnp.broadcast_to(ab_re, bu_re.shape)
    a_im = jnp.broadcast_to(ab_im, bu_im.shape)

    def combine(e1, e2):
        a1r, a1i, b1r, b1i = e1
        a2r, a2i, b2r, b2i = e2
        return (a2r * a1r - a2i * a1i,
                a2r * a1i + a2i * a1r,
                a2r * b1r - a2i * b1i + b2r,
                a2r * b1i + a2i * b1r + b2i)

    _, _, h_re, h_im = lax.associative_scan(combine, (a_re, a_im, bu_re, bu_im), axis=1)
    y = (jnp.einsum('blgp,gcp->blgc', h_re, c_re.astype(jnp.float32))
         - jnp.einsum('blgp,gcp->blgc', h_im, c_im.astype(jnp.float32)))
    y = y + d_skip.astype(jnp.float32).reshape(SSM_GROUPS, SSM_GROUP) * uf
    return y.reshape(B, L, SSM_WIDTH).astype(u.dtype)

def first_inputs(seed: int = 0) -> dict:
    key = jax.random.key(seed)
    ks = jax.random.split(key, 24)
    f32 = jnp.float32
    nrm = lambda k, shape, scale: jax.random.normal(k, shape, f32) * scale
    n_idx = jnp.arange(SSM_STATE, dtype=f32)
    return {
        "x": jax.random.normal(ks[0], (BATCH, SEQ, D_MODEL), f32),
        "norm_mix_pre": 1.0 + nrm(ks[1], (DEPTH, D_MODEL), 0.05),
        "norm_mix_post": 1.0 + nrm(ks[2], (DEPTH, D_MODEL), 0.05),
        "norm_mlp_pre": 1.0 + nrm(ks[3], (DEPTH, D_MODEL), 0.05),
        "norm_mlp_post": 1.0 + nrm(ks[4], (DEPTH, D_MODEL), 0.05),
        "w_in": nrm(ks[5], (DEPTH, D_MODEL, IN_WIDTH), D_MODEL ** -0.5),
        "rel_bias": nrm(ks[6], (N_BUCKETS, N_Q_HEADS), 0.5),
        "sinks": nrm(ks[7], (DEPTH, N_Q_HEADS), 0.5),
        "lam_re": -0.5 + nrm(ks[8], (DEPTH, SSM_GROUPS, SSM_STATE), 0.02),
        "lam_im": math.pi * n_idx + nrm(ks[9], (DEPTH, SSM_GROUPS, SSM_STATE), 0.02),
        "log_dt": jax.random.uniform(ks[10], (DEPTH, SSM_GROUPS), f32,
                                     math.log(DT_MIN), math.log(DT_MAX)),
        "b_re": nrm(ks[11], (DEPTH, SSM_GROUPS, SSM_STATE, SSM_GROUP), SSM_GROUP ** -0.5),
        "b_im": nrm(ks[12], (DEPTH, SSM_GROUPS, SSM_STATE, SSM_GROUP), SSM_GROUP ** -0.5),
        "c_re": nrm(ks[13], (DEPTH, SSM_GROUPS, SSM_GROUP, SSM_STATE), SSM_STATE ** -0.5),
        "c_im": nrm(ks[14], (DEPTH, SSM_GROUPS, SSM_GROUP, SSM_STATE), SSM_STATE ** -0.5),
        "d_skip": nrm(ks[15], (DEPTH, SSM_WIDTH), 1.0),
        "w_glu": nrm(ks[16], (DEPTH, SSM_WIDTH, SSM_WIDTH), SSM_WIDTH ** -0.5),
        "w_attn_branch": nrm(ks[17], (DEPTH, ATTN_WIDTH, D_MODEL), ATTN_WIDTH ** -0.5),
        "w_ssm_branch": nrm(ks[18], (DEPTH, SSM_WIDTH, D_MODEL), SSM_WIDTH ** -0.5),
        "w_out": nrm(ks[19], (DEPTH, D_MODEL, D_MODEL), D_MODEL ** -0.5),
        "w_ff_in": nrm(ks[20], (DEPTH, D_MODEL, D_FF), D_MODEL ** -0.5),
        "w_ff_out": nrm(ks[21], (DEPTH, D_FF, D_MODEL), D_FF ** -0.5),
    }

def first_block(x, norm_mix_pre, norm_mix_post, norm_mlp_pre, norm_mlp_post, w_in, rel_bias,
              sinks, lam_re, lam_im, log_dt, b_re, b_im, c_re, c_im, d_skip, w_glu,
              w_attn_branch, w_ssm_branch, w_out, w_ff_in, w_ff_out):
    B, L = x.shape[0], x.shape[1]
    for l in range(DEPTH):
        h = rmsnorm(x, norm_mix_pre[l])
        proj = h @ w_in[l]
        q, k, v, u, g_attn, g_ssm = jnp.split(proj, SPLITS, axis=-1)
        q = q.reshape(B, L, N_Q_HEADS, HEAD_DIM)
        k = k.reshape(B, L, N_KV_HEADS, HEAD_DIM)
        v = v.reshape(B, L, N_KV_HEADS, HEAD_DIM)
        y_attn = sliding_window_attention(q, k, v, sinks[l], rel_bias) @ w_attn_branch[l]
        z = jax.nn.gelu(s5_ssm(u, lam_re[l], lam_im[l], log_dt[l], b_re[l], b_im[l],
                               c_re[l], c_im[l], d_skip[l]))
        z = z * jax.nn.sigmoid(z @ w_glu[l])
        y_ssm = z @ w_ssm_branch[l]
        merged = jax.nn.sigmoid(g_attn) * y_attn + jax.nn.sigmoid(g_ssm) * y_ssm
        x = x + rmsnorm(merged @ w_out[l], norm_mix_post[l])
        h = rmsnorm(x, norm_mlp_pre[l])
        f = jnp.square(jax.nn.relu(h @ w_ff_in[l])) @ w_ff_out[l]
        x = x + rmsnorm(f, norm_mlp_post[l])
    return x


CHUNK = 128
A_GROUPS = 8
A_WIDTH = 512
A_HEAD = A_WIDTH // A_GROUPS
B_WIDTH = 512
CONV_WIDTH = 3
C_WIDTH = 512
POOL_WINDOWS = (2, 4, 8, 16)
C_GROUP = C_WIDTH // len(POOL_WINDOWS)
IN_TOTAL = 3 * A_WIDTH + 4 * B_WIDTH + 2 * C_WIDTH + 3 * D_MODEL
LN_EPS = 1e-5


def _rmsnorm(x, g):
    xf = x.astype(jnp.float32)
    y = xf * lax.rsqrt(jnp.mean(xf * xf, axis=-1, keepdims=True) + RMS_EPS)
    return (y * g.astype(jnp.float32)).astype(x.dtype)

def _layernorm(x, g, b):
    xf = x.astype(jnp.float32)
    mu = jnp.mean(xf, axis=-1, keepdims=True)
    xc = xf - mu
    var = jnp.mean(xc * xc, axis=-1, keepdims=True)
    y = xc * lax.rsqrt(var + LN_EPS)
    return (y * g.astype(jnp.float32) + b.astype(jnp.float32)).astype(x.dtype)

def _split_points():
    widths = [A_WIDTH] * 3 + [B_WIDTH] * 4 + [C_WIDTH] * 2 + [D_MODEL] * 3
    return [int(s) for s in np.cumsum(widths)[:-1]]

def _gmlp_branch(u, v, ln_g, ln_b, w_s, b_s):
    u = jax.nn.gelu(u)
    v = _layernorm(jax.nn.gelu(v), ln_g, ln_b)
    bsz, s, _ = v.shape
    vc = v.reshape(bsz, s // CHUNK, CHUNK, A_GROUPS, A_HEAD)
    causal = jnp.tril(jnp.ones((CHUNK, CHUNK), dtype=bool))
    w_m = jnp.where(causal, w_s, 0.0)
    sg = jnp.einsum('gts,bnsgc->bntgc', w_m, vc) + b_s.T[:, :, None]
    return u * sg.reshape(bsz, s, A_WIDTH)

def _shortconv_branch(xb, bg, cg, conv_w, conv_b):
    y = cg * xb
    y = lax.conv_general_dilated(
        y, conv_w[:, None, :].astype(y.dtype), window_strides=(1,),
        padding=[(CONV_WIDTH - 1, 0)], dimension_numbers=('NWC', 'WIO', 'NWC'),
        feature_group_count=B_WIDTH) + conv_b
    return bg * y

def _pool_branch(xc, w_pool, pool_scale):
    bsz, s, _ = xc.shape
    xf = xc.astype(jnp.float32).reshape(bsz, s, len(POOL_WINDOWS), C_GROUP)
    cs = jnp.cumsum(xf, axis=1)
    t_count = jnp.arange(1, s + 1, dtype=jnp.float32)
    pooled = []
    for gi, w in enumerate(POOL_WINDOWS):
        c = cs[:, :, gi]
        lag = jnp.pad(c[:, :s - w], ((0, 0), (w, 0), (0, 0)))
        cnt = jnp.minimum(t_count, float(w))[None, :, None]
        pooled.append((c - lag) / cnt)
    pooled = (jnp.stack(pooled, axis=2) - xf).astype(xc.dtype)
    y = jnp.einsum('bsgc,gcd->bsgd', pooled, w_pool).reshape(bsz, s, C_WIDTH)
    return y * pool_scale

def _hybrid_layer(x, norm_g, w_in, ln_g, ln_b, w_s, b_s, conv_w, conv_b,
                  w_pool, pool_scale, w_pa, w_pb, w_pc, w_o):
    h = _rmsnorm(x, norm_g)
    p = h @ w_in
    (u, v, z_a, x_b, b_g, c_g, z_b, x_c, z_c,
     g_a, g_b, g_c) = jnp.split(p, _split_points(), axis=-1)
    y_a = (_gmlp_branch(u, v, ln_g, ln_b, w_s, b_s) * jax.nn.silu(z_a)) @ w_pa
    y_b = (_shortconv_branch(x_b, b_g, c_g, conv_w, conv_b) * jax.nn.silu(z_b)) @ w_pb
    y_c = (_pool_branch(x_c, w_pool, pool_scale) * jax.nn.silu(z_c)) @ w_pc
    merged = (jax.nn.sigmoid(g_a) * y_a + jax.nn.sigmoid(g_b) * y_b
              + jax.nn.sigmoid(g_c) * y_c)
    return x + merged @ w_o

def second_inputs(seed: int = 0) -> dict:
    key = jax.random.key(seed)
    ks = jax.random.split(key, 20)
    f32 = jnp.float32
    n = lambda k, shape: jax.random.normal(k, shape, dtype=f32)
    return {
        "x": n(ks[0], (BATCH, SEQ, D_MODEL)),
        "norm_g": 1.0 + 0.02 * n(ks[1], (DEPTH, D_MODEL)),
        "w_in": n(ks[2], (DEPTH, D_MODEL, IN_TOTAL)) * D_MODEL ** -0.5,
        "ln_g": 1.0 + 0.02 * n(ks[3], (DEPTH, A_WIDTH)),
        "ln_b": 0.02 * n(ks[4], (DEPTH, A_WIDTH)),
        "w_s": n(ks[5], (DEPTH, A_GROUPS, CHUNK, CHUNK)) * CHUNK ** -0.5,
        "b_s": 1.0 + 0.1 * n(ks[6], (DEPTH, A_GROUPS, CHUNK)),
        "conv_w": n(ks[7], (DEPTH, CONV_WIDTH, B_WIDTH)) * CONV_WIDTH ** -0.5,
        "conv_b": 0.02 * n(ks[8], (DEPTH, B_WIDTH)),
        "w_pool": n(ks[9], (DEPTH, len(POOL_WINDOWS), C_GROUP, C_GROUP)) * C_GROUP ** -0.5,
        "pool_scale": 1.0 + 0.02 * n(ks[10], (DEPTH, C_WIDTH)),
        "w_pa": n(ks[11], (DEPTH, A_WIDTH, D_MODEL)) * A_WIDTH ** -0.5,
        "w_pb": n(ks[12], (DEPTH, B_WIDTH, D_MODEL)) * B_WIDTH ** -0.5,
        "w_pc": n(ks[13], (DEPTH, C_WIDTH, D_MODEL)) * C_WIDTH ** -0.5,
        "w_o": n(ks[14], (DEPTH, D_MODEL, D_MODEL)) * D_MODEL ** -0.5,
        "final_g": 1.0 + 0.02 * n(ks[15], (D_MODEL,)),
    }

def second_block(x, norm_g, w_in, ln_g, ln_b, w_s, b_s, conv_w, conv_b, w_pool,
              pool_scale, w_pa, w_pb, w_pc, w_o, final_g):
    for l in range(DEPTH):
        x = _hybrid_layer(x, norm_g[l], w_in[l], ln_g[l], ln_b[l], w_s[l], b_s[l],
                          conv_w[l], conv_b[l], w_pool[l], pool_scale[l],
                          w_pa[l], w_pb[l], w_pc[l], w_o[l])
    return _rmsnorm(x, final_g)


_first_inputs = second_inputs


def second_inputs(seed=0):
    import zlib

    import numpy as np

    out = dict(_first_inputs(seed))
    spreads = {}
    factors = {'norm_g': 3.328,
     'ln_g': 8.0,
     'ln_b': 8.0,
     'b_s': 2.889,
     'conv_b': 8.0,
     'pool_scale': 8.0,
     'final_g': 2.862}
    for name, (base, spread) in spreads.items():
        noise = np.random.default_rng([zlib.crc32(name.encode()), seed]).standard_normal(out[name].shape)
        drawn = base * np.exp(spread * noise) if base else spread * noise
        out[name] = __import__('jax').numpy.asarray(drawn.astype(out[name].dtype))
    for name, factor in factors.items():
        out[name] = (out[name] * factor).astype(out[name].dtype)
    return out


_narrow_inputs = second_inputs


def second_inputs(seed=0):

    out = dict(_narrow_inputs(seed))
    wider = {'ln_g': 11.51,
     'ln_b': 11.61,
     'b_s': 3.97,
     'conv_b': 5.62,
     'pool_scale': 5.78,
     'final_g': 3.22}
    for name, times in wider.items():
        mean = out[name].mean()
        out[name] = (mean + times * (out[name] - mean)).astype(out[name].dtype)
    return out


def setup_inputs(seed=0):
    out = dict(first_inputs(seed))
    for name, value in second_inputs(seed + 1).items():
        if name != "x":
            out[name + "_2"] = value
    return out


def reference(
    x, norm_mix_pre, norm_mix_post, norm_mlp_pre, norm_mlp_post, w_in, rel_bias, sinks, lam_re,
    lam_im, log_dt, b_re, b_im, c_re, c_im, d_skip, w_glu, w_attn_branch, w_ssm_branch, w_out,
    w_ff_in, w_ff_out, norm_g_2, w_in_2, ln_g_2, ln_b_2, w_s_2, b_s_2, conv_w_2, conv_b_2,
    w_pool_2, pool_scale_2, w_pa_2, w_pb_2, w_pc_2, w_o_2, final_g_2,
):
    x = first_block(
        x, norm_mix_pre, norm_mix_post, norm_mlp_pre, norm_mlp_post, w_in, rel_bias, sinks,
        lam_re, lam_im, log_dt, b_re, b_im, c_re, c_im, d_skip, w_glu, w_attn_branch,
        w_ssm_branch, w_out, w_ff_in, w_ff_out,
    )
    return second_block(
        x, norm_g_2, w_in_2, ln_g_2, ln_b_2, w_s_2, b_s_2, conv_w_2, conv_b_2, w_pool_2,
        pool_scale_2, w_pa_2, w_pb_2, w_pc_2, w_o_2, final_g_2,
    )


_drawn_inputs = setup_inputs


def setup_inputs(seed=0):
    import zlib

    import numpy as np

    out = dict(_drawn_inputs(seed))
    spreads = {}
    factors = {'sinks': 6.553, 'lam_re': 8.0}
    for name, (base, spread) in spreads.items():
        noise = np.random.default_rng([zlib.crc32(name.encode()), seed]).standard_normal(out[name].shape)
        drawn = base * np.exp(spread * noise) if base else spread * noise
        out[name] = __import__('jax').numpy.asarray(drawn.astype(out[name].dtype))
    for name, factor in factors.items():
        out[name] = (out[name] * factor).astype(out[name].dtype)
    return out
```

```python
import concourse.bass as bass
from concourse import mybir
from contextlib import ExitStack
import numpy as np

P = 128
SEQ, D = 1024, 1024
KD = D // P
MT = SEQ // P
HEADS, KV, HD = 8, 2, 64
BUCKETS, WINDOW, MAXD = 32, 128, 128
G, C, NS = 32, 16, 64
TAU = 8
CH = SEQ // TAU
PAIRS = G // 2
W4 = 512
KW = W4 // P
FF = 4096
FCH = FF // W4
CONV = 3
POOLS = (2, 4, 8, 16)
RMS_EPS, LN_EPS = 1e-6, 1e-5
NEG = -1e30
ROWLEN = 3 * P

STAGES = [("q", 4, 8), ("kv", 2, 8), ("gate1", 16, 8), ("u", 4, 8), ("glu", 4, 4), ("merge1", 16, 4),
          ("wout", 8, 8), ("ff", 12 * FCH, 0), ("v2", 4, 8), ("au", 4, 8), ("az", 4, 8), ("amerge", 16, 0),
          ("bx", 4, 8), ("bc", 4, 8), ("bb", 4, 8), ("bz", 4, 8), ("bmerge", 16, 0),
          ("cx", 4, 8), ("cz", 4, 8), ("pool", 4, 1), ("cmerge", 16, 0)]
START, KOF = {}, []
for _name, _n, _k in STAGES:
    START[_name] = len(KOF)
    if _name == "ff":
        KOF += ([8] * 4 + [4] * 8) * FCH
    elif _k == 0:
        KOF += [8, 8, 4, 4] * 4
    else:
        KOF += [_k] * _n
NT = len(KOF)
A_U, A_V, A_Z, B_X, B_B, B_C, B_Z, C_X, C_Z, G_A, G_B, G_C = [0, 512, 1024, 1536, 2048, 2560, 3072, 3584, 4096,
                                                              4608, 5632, 6656]


def bucket_rows():
    rows = np.zeros((BUCKETS + 1, ROWLEN), np.float32)
    half = BUCKETS // 2
    for m in range(ROWLEN):
        d = 2 * P - 1 - m
        if not 0 <= d < WINDOW:
            rows[BUCKETS, m] = 1.0
            continue
        b = d
        if d >= half:
            b = min(half + int(np.log(d / half) / np.log(MAXD / half) * (BUCKETS - half)), BUCKETS - 1)
        rows[b, m] = 1.0
    return rows


def hybrid_kernel(nc, io, out):
    f32, f32r = mybir.dt.float32, mybir.dt.float32r
    ALU, ACT, AX = mybir.AluOpType, mybir.ActivationFunctionType, mybir.AxisListType
    ds = bass.ds
    KB = 1024
    ctx = ExitStack()
    with ctx:
        arena = ctx.enter_context(nc.sbuf_tensor("arena", [P, 207 * 256], f32))
        ORIGIN = nc.sbuf_base - 207 * KB

        def at(name, shape, kib, dt=f32):
            return nc.alloc_sbuf_tensor_at(name, shape, dt, offset=ORIGIN + int(kib * KB))

        def sem(name):
            return ctx.enter_context(nc.semaphore(name))

        def dram(name, shape):
            return nc.dram_tensor(name, shape, f32, kind="Internal").ap()

        raw = at("raw", [P, 2, KD, 2 * P], 0)
        WH = at("WH", [P, 2, KD, P], 16, f32r)
        WL = at("WL", [P, 2, KD, P], 24, f32r)
        vec = at("vec", [P, 448], 32)
        RA = at("RA", [P, SEQ], 34)
        RP = at("RP", [P, SEQ], 38)
        ACC = at("ACC", [P, SEQ], 42)
        S = at("S", [P, 2, SEQ], 46)
        ident = at("ident", [P, P], 54)
        ones = at("ones", [P, P], 54.5)
        small = at("small", [P, 256], 55)
        XH, XL = at("XH", [P, KD, SEQ], 56, f32r), at("XL", [P, KD, SEQ], 88, f32r)
        XT = at("XT", [P, KD, SEQ], 120)
        xtok = at("xtok", [P, MT, D], 152)
        q, k_, v = at("q", [P, 4, SEQ], 120), at("k", [P, SEQ], 136), at("v", [P, MT, P], 140)
        gst = at("gst", [P, 2, SEQ], 184)
        ust = at("ust", [P, 2, SEQ], 192)
        AOH, AOL = at("AOH", [P, KW, SEQ], 56, f32r), at("AOL", [P, KW, SEQ], 72, f32r)
        bias = at("bias", [P, HEADS, 2 * P], 88)
        prob = at("prob", [P, 2, 4, 2 * P], 96)
        probT = at("probT", [P, 2, 8, P], 104)
        otok = at("otok", [P, 2, 2 * P], 112)
        bsel = at("bsel", [BUCKETS + 1, ROWLEN], 200)
        rel = at("rel", [BUCKETS + 1, HEADS], 202)
        brow = at("brow", [HEADS, ROWLEN], 203)
        U = at("U", [P, G, CH], 88)
        ETr, ETi = at("ETr", [P, PAIRS, P], 104), at("ETi", [P, PAIRS, P], 112)
        Lm = at("Lm", [P, G, P], 120)
        FXr, FXi = at("FXr", [P, PAIRS, TAU + 1, C], 136), at("FXi", [P, PAIRS, TAU + 1, C], 145)
        RC, RS = at("RC", [P, PAIRS, CH], 154), at("RS", [P, PAIRS, CH], 162)
        Dk = at("Dk", [P, PAIRS, CH], 170)
        Kt = at("Kt", [32, PAIRS, P], 170)
        Vr, Vi = at("Vr", [P, PAIRS, CH], 178), at("Vi", [P, PAIRS, CH], 186)
        M1r, M1i = at("M1r", [P, PAIRS, TAU, C], 178), at("M1i", [P, PAIRS, TAU, C], 186)
        Br, Bi = at("Br", [P, PAIRS, C], 194), at("Bi", [P, PAIRS, C], 195)
        Cn = at("Cn", [P, 2, 4, 2, NS], 196)
        Cr, Ci = at("Cr", [P, PAIRS, C], 200), at("Ci", [P, PAIRS, C], 201)
        BBr, BBi = at("BBr", [P, PAIRS, 2, C], 202), at("BBi", [P, PAIRS, 2, C], 204)
        dsk = at("dsk", [32, PAIRS], 206)
        eye16 = at("eye16", [32, C], 206.25)
        lam = at("lam", [P, 64, PAIRS], 46)
        Ar, Ai = at("Ar", [P, TAU + 1, PAIRS], 50), at("Ai", [P, TAU + 1, PAIRS], 51)
        Bbr, Bbi = at("Bbr", [P, PAIRS, C], 52), at("Bbi", [P, PAIRS, C], 53)
        ct = at("ct", [P, 4, 256], 42)
        rt = at("rt", [P, 2, PAIRS * CH // 2], 178)
        Hr, Hi = at("Hr", [P, PAIRS, CH], 104), at("Hi", [P, PAIRS, CH], 112)
        Ysb = at("Ysb", [P, G, CH], 178)
        Z = at("Z", [P, KW, SEQ], 88)
        ZH, ZL = at("ZH", [P, KW, SEQ], 104, f32r), at("ZL", [P, KW, SEQ], 120, f32r)
        Z2H, Z2L = at("Z2H", [P, KW, SEQ], 136, f32r), at("Z2L", [P, KW, SEQ], 152, f32r)
        gin = at("gin", [P, 4, SEQ], 120)
        MH, ML = at("MH", [P, KD, SEQ], 88, f32r), at("ML", [P, KD, SEQ], 168, f32r)
        F = at("F", [P, KD, SEQ], 56)
        YH, YL = at("YH", [P, KD, SEQ], 88, f32r), at("YL", [P, KD, SEQ], 120, f32r)
        xr1 = at("xr1", [P, 3, SEQ], 152)
        HH, HL = at("HH", [P, KW, SEQ], 152, f32r), at("HL", [P, KW, SEQ], 168, f32r)
        xr2 = at("xr2", [P, 3, SEQ], 184)
        V2 = at("V2", [P, MT, W4], 56)
        wst = at("wst", [P, 8, P], 72)
        lng, lnb = at("lng", [P, W4], 80), at("lnb", [P, W4], 82)
        bsb = at("bsb", [P, KW, P], 84)
        wsr = at("wsr", [P, 8, P], 152)
        M = at("M", [P, KD, SEQ], 56)
        BH, BL = at("BH", [P, KW, SEQ], 152, f32r), at("BL", [P, KW, SEQ], 168, f32r)
        Y = at("Y", [P, KW, SEQ], 184)
        Gb = [ACC, at("G1", [P, SEQ], 200)]
        cnt = at("cnt", [P, KW, 16], 204)
        WOH, WOL = at("WOH", [P, KD, D], 88, f32r), at("WOL", [P, KD, D], 120, f32r)
        NH, NL = at("NH", [P, KD, SEQ], 152, f32r), at("NL", [P, KD, SEQ], 56, f32r)
        xr3 = at("xr3", [P, 3, KD, P], 184)
        fgb = at("fgb", [P, D], 196)

        def column(n, at_=[0]):
            at_[0] += n
            return vec[:, at_[0] - n:at_[0]]

        g_pre1, g_post1, g_pre2, g_post2, g_pre3 = [column(KD) for _ in range(5)]
        cw, cb, psc = column(CONV * KW), column(KW), column(KW)
        sink = column(HEADS)
        one_col, half_neg = column(1), column(KD)
        ms, rtok = column(KD), column(KD)
        mx, nm, den, es, rd = [column(8) for _ in range(5)]
        bn, ag, lnr = column(6), column(2), column(1)
        lnv = column(1)
        ss, fv, fr = column(MT), column(MT), column(MT)

        acc = [ctx.enter_context(nc.psum_tensor(f"acc{i}", [P, 1024], f32)) for i in range(2)]
        aux = [ctx.enter_context(nc.psum_tensor(f"aux{i}", [P, 1024], f32)) for i in range(2)]

        x_scr = [dram(f"x_scr{i}", [D, SEQ]) for i in range(3)]
        g_scr = dram("g_scr", [16 * P, SEQ])
        u_scr, y_scr = dram("u_scr", [W4, SEQ]), dram("y_scr", [W4, SEQ])
        b_scr = dram("b_scr", [HEADS, P, ROWLEN])

        w_in_s = [sem("w_loaded0"), sem("w_loaded1")]
        w_hi, w_lo, tile_done = sem("w_hi"), sem("w_lo"), sem("tile_done")
        evicted = [sem("evicted0"), sem("evicted1")]
        c_in, id_in, bs_in = sem("constants_loaded"), sem("identity_loaded"), sem("bucket_rows_loaded")
        x_in = [sem(f"x{m}_loaded") for m in range(MT)]
        xt_ready, xt_a, xt_d = sem("xt_ready"), sem("xt_evicted_act"), sem("xt_evicted_dve")
        ones_set, const_set = sem("ones_set"), sem("const_set")
        xh_ready, xl_ready = sem("xh_ready"), sem("xl_ready")
        sq_ready, sq_added = sem("sq_ready"), sem("sq_added")
        mean_ready, ms_ready, rtok_ready = sem("mean_ready"), sem("ms_ready"), sem("rtok_ready")
        rdg_ready, rb_ready, r_ready = sem("rdiag_ready"), sem("rb_ready"), sem("r_ready")
        x_out = sem("residual_stored")
        dchain, pchain, achain = sem("dve_chain"), sem("pool_chain"), sem("act_chain")
        g_pre, g_post = sem("gate_scaled"), sem("gate_ready")
        g_out = [sem("gate_stored0"), sem("gate_stored1")]
        u_out, u_in = [sem("u_stored0"), sem("u_stored1")], sem("u_loaded")
        b_row, b_rowsb, b_out, b_in = sem("b_row"), sem("b_row_copied"), sem("b_stored"), sem("b_loaded")
        s_ready, s_read, nm_ready, p_ready = sem("s_ready"), sem("s_read"), sem("nm_ready"), sem("p_ready")
        pt_ready, ptc, o_ready, o_read = sem("pt_ready"), sem("pt_copied"), sem("o_ready"), sem("o_read")
        aot_ready, aoh, aot_read = sem("aot_ready"), sem("ao_hi"), sem("ao_lo")
        par_in = sem("ssm_loaded")
        a1, a2, a3 = sem("dt_ready"), sem("angle_ready"), sem("trig_ready")
        ct_ready, c_ready = sem("c_transposed"), sem("c_copied")
        m1_ready, et_ready, et_copied = sem("m1_ready"), sem("et_ready"), sem("et_copied")
        k_ready, k_copied, l_zero, l_in = sem("k_ready"), sem("k_copied"), sem("l_zero"), sem("l_filled")
        x_ready, h_ready, yk_ready = sem("x_ready"), sem("h_ready"), sem("yk_ready")
        y_sb = sem("y_copied")
        y_out, z_in = sem("y_stored"), sem("z_loaded")
        z_act, zh_ready, zl_ready = sem("z_act"), sem("zh_ready"), sem("zl_ready")
        glu_sig, glu_mul, z2h, z2l = sem("glu_sig"), sem("glu_mul"), sem("z2_hi"), sem("z2_lo")
        ga_in = [sem(f"gin{i}") for i in range(4)]
        m_sum, mh_ready, ml_ready = sem("m_sum"), sem("mh_ready"), sem("ml_ready")
        ya_done, ys_done = sem("ya_done"), sem("ys_done")
        f_out = sem("f_evicted")
        f_scaled, x_added = sem("f_scaled"), sem("x_added")
        xr_in = [sem(f"xr{i}_loaded") for i in range(3)]
        f_zero, f_added, f_final = sem("f_zero"), sem("f_added"), sem("f_final")
        relu_done, hsq, hh, hl = sem("relu_done"), sem("hidden_squared"), sem("hidden_hi"), sem("hidden_lo")
        v2_done, v2_gelu, ln_var, ln_r, ln_done = sem("v2_done"), sem("v2_gelu"), sem("ln_var"), sem("ln_r"), sem("ln_done")
        p2_in, ws_t, ws_c, ws_m = sem("p2_loaded"), sem("ws_t"), sem("ws_copied"), sem("ws_masked")
        sA, uA, gA, yA = sem("a_scaled"), sem("a_gelu"), sem("a_silu"), sem("a_product")
        sg_ready, sg_add, sg_mul = sem("sg_ready"), sem("sg_added"), sem("sg_mul")
        bh, bl = sem("branch_hi"), sem("branch_lo")
        mg_s, mg_g, mg_y, mg_m = sem("mg_scaled"), sem("mg_gate"), sem("mg_product"), sem("mg_added")
        b1, b2, b3, b4, b5, b6 = [sem(f"b_step{i}") for i in range(6)]
        c1, c2, c3 = sem("c_scaled"), sem("c_silu"), sem("c_mixed")
        nh, nl, wo_hi, wo_lo = sem("nh_ready"), sem("nl_ready"), sem("wo_hi"), sem("wo_lo")
        p_in, fsum, fv_r, fr_r, o_done = sem("fg_loaded"), sem("out_sum"), sem("fv"), sem("fr"), sem("out_ready")
        ot_ready = sem("ot_ready")
        stored = [sem("stored0"), sem("stored1")]
        x3_in = [sem(f"x3_{i}") for i in range(3)]

        block = ctx.enter_context(nc.Block())

        def row(t, f):
            return t[:, f, :] if isinstance(f, int) else t[:, ds(f, 1), :].rearrange("p o n -> p (o n)")

        def perm(t):
            return t.rearrange("p (h t) -> p t h", t=TAU)

        def unperm(t):
            return t.rearrange("p (t h) -> p t h", t=TAU)

        def repeat(eng, n, body):
            body(0)
            with eng.Fori(1, n - 1) as i:
                body(i)
            body(n - 1)

        def plus(base, per, i):
            return base + per * i

        def first_turn(i):
            return isinstance(i, int) and i == 0

        def ev(T0):
            return evicted[T0 % 2]

        def ev_wait(eng, T0, per=0, i=0):
            eng.wait_ge(evicted[T0 % 2], plus(T0 // 2 + 1, per // 2, i))

        @block.sync
        def _(sp):
            def panel(p0, src, kb, per=0, i=0):
                if p0 >= 2:
                    sp.wait_ge(w_lo, plus(2 * (p0 - 1), 2 * per, i))
                sp.dma_start(raw[:, p0 % 2, 0:kb, :], src).then_inc(w_in_s[p0 % 2], 16)

            def cols(w, c, n=2 * P):
                return w[:, :, ds(c, n)] if not isinstance(c, int) else w[:, :, c:c + n]

            w1 = io["w_in"].rearrange("o (k p) n -> p (o k) n", p=P)
            w2 = io["w_in_2"].rearrange("o (k p) n -> p (o k) n", p=P)
            xt_ = io["x"].rearrange("b (m p) d -> p (b m) d", p=P)
            for m in range(MT):
                sp.dma_start(xtok[:, m, :], xt_[:, m, :]).then_inc(x_in[m], 16)
                if m == 3:
                    qw = io["w_in"][:, :, 0:512].rearrange("o (k p) (a j d) -> a j p (o k) d", p=P, a=2, d=HD)
                    for pp in range(2):
                        for j in range(2):
                            for a in range(2):
                                sp.dma_start(raw[:, pp, :, j * P + a * HD:j * P + (a + 1) * HD],
                                             qw[a, 2 * pp + j]).then_inc(w_in_s[pp], 16)
            panel(START["kv"] // 2, cols(w1, 512), 8)
            G0 = 512 + 2 * P + W4

            def gate_panels(i):
                for h in range(2):
                    panel(START["gate1"] // 2 + h, cols(w1, plus(G0 + h * 256, 512, i)), 8, 2, i)
            for i in range(4):
                gate_panels(i)
            for h in range(2):
                panel(START["u"] // 2 + h, cols(w1, 768 + 256 * h), 8)
            sp.wait_ge(tile_done, START["u"] + 4)
            sp.wait_ge(b_out, 16)
            sp.dma_start(bias[:], bass.AP(b_scr.tensor, P - 1, [[ROWLEN - 1, P], [P * ROWLEN, HEADS], [1, 2 * P]])
                         ).then_inc(b_in, 16)
            wg = io["w_glu"].rearrange("o (k p) n -> p (o k) n", p=P)
            for h in range(2):
                panel(START["glu"] // 2 + h, cols(wg, 256 * h), 4)
            with nc.allow_non_contiguous_dma("small parameters"):
                for n in range(2):
                    sp.wait_ge(u_out[n], 32)
                for g2 in range(2):
                    dst = slice(g2 * NS, (g2 + 1) * NS)
                    sp.dma_start(Br[dst], io["b_re"].rearrange("o (a b) s c -> (o b) s a c", b=2)[g2]).then_inc(par_in, 16)
                    sp.dma_start(Bi[dst], io["b_im"].rearrange("o (a b) s c -> (o b) s a c", b=2)[g2]).then_inc(par_in, 16)
                for n, name in enumerate(("c_re", "c_im")):
                    for dup in range(2):
                        sp.dma_start(Cn[:, n, :, dup, :], io[name].rearrange("o (t g) c s -> (g c) (o t) s", g=8)
                                     ).then_inc(par_in, 16)
                sp.wait_ge(g_post, 16)
                for g2 in range(2):
                    dst = slice(g2 * NS, (g2 + 1) * NS)
                    for n, name in enumerate(("lam_re", "lam_im")):
                        sp.dma_start(lam[dst, n, :], io[name].rearrange("o (a b) s -> (o b) s a", b=2)[g2]
                                     ).then_inc(par_in, 16)
                    sp.dma_start(lam[dst, 2, :], bass.AP(io["log_dt"].tensor, g2, [[0, NS], [2, PAIRS]])
                                 ).then_inc(par_in, 16)
                    sp.dma_start(dsk[g2 * C:(g2 + 1) * C, :],
                                 io["d_skip"].rearrange("o (a b c) -> (o b) c a", b=2, c=C)[g2]).then_inc(par_in, 16)
            sp.dma_start(eye16[:], io["eye16"]).then_inc(par_in, 16)
            sp.wait_ge(s_read, 16)
            sp.wait_ge(pt_ready, 16)
            uv = u_scr.rearrange("(g c) (t h) -> t c g h", c=C, t=TAU)
            for t in range(TAU):
                sp.dma_start(U[t * C:(t + 1) * C], uv[t]).then_inc(u_in, 16)
            sp.wait_ge(l_zero, 1)
            sp.wait_ge(k_copied, 1)
            Lv = Lm[:].rearrange("p (a b) m -> p a b m", b=2)
            for t in range(TAU):
                for g2 in range(2):
                    sp.dma_start(Lv[t * C:(t + 1) * C, :, g2, t * C:P], Kt[g2 * C:(g2 + 1) * C, :, 0:P - t * C]
                                 ).then_inc(l_in, 16)
            sp.wait_ge(y_sb, 4)
            yv = y_scr.rearrange("(g c) (t h) -> t c g h", c=C, t=TAU)
            for t in range(TAU):
                sp.dma_start(yv[t], Ysb[t * C:(t + 1) * C]).then_inc(y_out, 16)
            sp.wait_ge(y_out, 16 * TAU)
            for t in range(KW):
                sp.dma_start(Z[:, t, :], y_scr[t * P:(t + 1) * P, :]).then_inc(z_in, 16)
            wa = io["w_attn_branch"].rearrange("o (k p) n -> p (o k) n", p=P)
            wsb = io["w_ssm_branch"].rearrange("o (k p) n -> p (o k) n", p=P)
            gv = g_scr.rearrange("(f p) t -> p f t", p=P)
            sp.wait_ge(g_out[0], 16 * 8)
            sp.wait_ge(g_out[1], 16 * 8)
            sp.wait_ge(tile_done, START["merge1"])

            def merge_loads(i):
                panel(START["merge1"] // 2, cols(wa, plus(0, 256, i)), 4, 2, i)
                for h in range(2):
                    for n in range(2):
                        ev_wait(sp, START["merge1"] - 4 + 2 * n + h, 4, i)
                        f = plus(n * 8 + h, 2, i)
                        sp.dma_start(gin[:, 2 * n + h, :], row(gv, f)).then_inc(ga_in[2 * n + h], 16)
                panel(START["merge1"] // 2 + 1, cols(wsb, plus(0, 256, i)), 4, 2, i)
            for i in range(4):
                merge_loads(i)
            wo1 = io["w_out"].rearrange("o (k p) n -> p (o k) n", p=P)
            for h in range(4):
                panel(START["wout"] // 2 + h, cols(wo1, 256 * h), 8)
            sp.wait_ge(tile_done, START["wout"])

            def residual(j, src, ring):
                sp.wait_ge(x_out, 16 * 8 * (j + 1))
                for f in range(KD):
                    n = 8 * j + f
                    if f >= 3:
                        sp.wait_ge(x_added, n - 2)
                    sp.dma_start(ring[:, f % 3, :], row(src.rearrange("(f p) t -> p f t", p=P), f)
                                 ).then_inc(xr_in[f % 3], 16)
            wf1 = io["w_ff_in"].rearrange("o (k p) n -> p (o k) n", p=P)
            wf2 = io["w_ff_out"].rearrange("o (c k p) n -> p (o c k) n", p=P, k=KW)
            panel(START["ff"] // 2, cols(wf1, 0), 8)
            residual(0, x_scr[0], xr1)

            def ff_panels(c):
                for h in range(1 if c == 0 else 0, 2):
                    panel(START["ff"] // 2 + h, cols(wf1, plus(256 * h, 512, c)), 8, 6, c)
                for h in range(4):
                    src = wf2[:, ds(c * KW, KW), 256 * h:256 * (h + 1)] if not isinstance(c, int) else \
                        wf2[:, c * KW:(c + 1) * KW, 256 * h:256 * (h + 1)]
                    panel(START["ff"] // 2 + 2 + h, src, 4, 6, c)
            for c in range(FCH):
                ff_panels(c)
            panel(START["v2"] // 2, cols(w2, A_V), 8)
            sp.wait_ge(f_final, 1)
            residual(1, x_scr[1], xr2)
            sp.wait_ge(tile_done, START["v2"])
            sp.dma_start(wsr[:], io["w_s_2"].rearrange("o g t s -> t (o g) s")).then_inc(p2_in, 16)
            panel(START["v2"] // 2 + 1, cols(w2, A_V + 256), 8)
            sp.wait_ge(xl_ready, 24)
            sp.wait_ge(sq_ready, 40)
            sp.wait_ge(x_out, 16 * 24)
            sp.dma_start(lng[:], bass.AP(io["ln_g_2"].tensor, 0, [[0, P], [1, W4]])).then_inc(p2_in, 16)
            sp.dma_start(cnt[:], bass.AP(io["window_scale"].tensor, 0, [[0, P], [1, KW * 16]]).rearrange(
                "p (t w) -> p t w", t=KW)).then_inc(p2_in, 16)
            sp.dma_start(lnb[:], bass.AP(io["ln_b_2"].tensor, 0, [[0, P], [1, W4]])).then_inc(p2_in, 16)
            for h in range(2):
                sp.dma_start(bsb[h * 64:(h + 1) * 64],
                             bass.AP(io["b_s_2"].tensor, h * P, [[0, 64], [2 * P, KW], [1, P]])).then_inc(p2_in, 16)
            for name, col in (("au", A_U), ("az", A_Z)):
                for h in range(2):
                    panel(START[name] // 2 + h, cols(w2, col + 256 * h), 8)

            def branch_panels(stage, gate_col, wname):
                wp = io[wname].rearrange("o (k p) n -> p (o k) n", p=P)

                def turn(i):
                    panel(START[stage] // 2, cols(w2, plus(gate_col, 256, i)), 8, 2, i)
                    panel(START[stage] // 2 + 1, cols(wp, plus(0, 256, i)), 4, 2, i)
                for i in range(4):
                    turn(i)
            branch_panels("amerge", G_A, "w_pa_2")
            for name, col in (("bx", B_X), ("bc", B_C), ("bb", B_B), ("bz", B_Z)):
                for h in range(2):
                    panel(START[name] // 2 + h, cols(w2, col + 256 * h), 8)
            branch_panels("bmerge", G_B, "w_pb_2")
            for name, col in (("cx", C_X), ("cz", C_Z)):
                for h in range(2):
                    panel(START[name] // 2 + h, cols(w2, col + 256 * h), 8)
            for h in range(2):
                p0 = START["pool"] // 2 + h
                sp.wait_ge(w_lo, 2 * (p0 - 1))
                sp.dma_start(raw[:, p0 % 2, 0, :].rearrange("p (g d) -> p g d", g=2),
                             io["w_pool_2"][0, 2 * h:2 * h + 2].rearrange("g c d -> c g d")).then_inc(w_in_s[p0 % 2], 16)
            branch_panels("cmerge", G_C, "w_pc_2")
            wo2 = io["w_o_2"].rearrange("o (k p) n -> p (o k) n", p=P)
            for i in range(4):
                p0 = NT // 2 + i
                if i < 2:
                    sp.wait_ge(w_lo, 2 * (p0 - 1))
                else:
                    sp.wait_ge(wo_lo, i - 1)
                sp.dma_start(raw[:, p0 % 2], cols(wo2, 256 * i)).then_inc(w_in_s[p0 % 2], 16)
            sp.wait_ge(tile_done, NT)
            sp.wait_ge(mg_m, 24)
            sp.dma_start(fgb[:], bass.AP(io["final_g_2"].tensor, 0, [[0, P], [1, D]])).then_inc(p_in, 16)
            x2v = x_scr[2].rearrange("(k p) (m t) -> m p k t", p=P, t=P)
            for m in range(3):
                sp.dma_start(xr3[:, m], x2v[m]).then_inc(x3_in[m], 16)
            for m in range(MT):
                if m + 3 < MT:
                    sp.wait_ge(ot_ready, m + 1)
                    sp.dma_start(xr3[:, m % 3], x2v[m + 3]).then_inc(x3_in[m % 3], 16)
                sp.wait_ge(o_done, m + 1)
                sp.dma_start(out[0, m * P:(m + 1) * P, :], S[:, m % 2, :]).then_inc(stored[m % 2], 16)
            for n in range(2):
                sp.wait_ge(stored[n], 8 * MT)

        @block.scalar
        def _(act):
            def w_count(T0):
                p0 = T0 // 2
                return 16 * (4 + p0 // 2)

            def hi(T0, per=0, i=0):
                if T0 >= NT:
                    return
                act.wait_ge(w_in_s[(T0 // 2) % 2], plus(w_count(T0), per // 4 * 16, i))
                if T0 >= 2:
                    act.wait_ge(tile_done, plus(T0 - 1, per, i))
                kb = KOF[T0]
                nc.scalar.activation(WH[:, T0 % 2, 0:kb, :],
                                     raw[:, (T0 // 2) % 2, 0:kb, (T0 % 2) * P:(T0 % 2 + 1) * P], ACT.Copy
                                     ).then_inc(w_hi, 1)

            def hi_next(T0, per, i):
                hi(T0 + 1 + per * i) if isinstance(i, int) else hi(T0 + 1, per, i)

            act.dma_start(ident[:], io["eye"]).then_inc(id_in, 16)
            act.dma_start(bsel[:], io["bucket_rows"]).then_inc(bs_in, 16)
            act.dma_start(rel[0:BUCKETS], io["rel_bias"]).then_inc(bs_in, 16)
            with nc.allow_non_contiguous_dma("small parameters"):
                for dst, name in ((g_pre1, "norm_mix_pre"), (g_post1, "norm_mix_post"), (g_pre2, "norm_mlp_pre"),
                                  (g_post2, "norm_mlp_post"), (g_pre3, "norm_g_2")):
                    act.dma_start(dst, io[name].rearrange("o (k p) -> p (o k)", p=P)).then_inc(c_in, 16)
                act.dma_start(cw.rearrange("p (j t) -> p j t", j=CONV),
                              io["conv_w_2"].rearrange("o j (t p) -> p (o j) t", p=P)).then_inc(c_in, 16)
                act.dma_start(cb, io["conv_b_2"].rearrange("o (t p) -> p (o t)", p=P)).then_inc(c_in, 16)
                act.dma_start(psc, io["pool_scale_2"].rearrange("o (t p) -> p (o t)", p=P)).then_inc(c_in, 16)
                act.dma_start(sink, bass.AP(io["sinks"].tensor, 0, [[0, P], [1, HEADS]])).then_inc(c_in, 16)

            for m in range(0, MT, 2):
                act.wait_ge(xt_ready, m + 1)
                nc.scalar.activation(XT[:, :, m * P:(m + 1) * P], aux[0][:].rearrange("p (k t) -> p k t", k=KD),
                                     ACT.Copy).then_inc(xt_a, 1)
            hi(0)
            act.wait_ge(b_row, 1)
            nc.scalar.activation(brow[:], aux[1][0:HEADS, 0:ROWLEN], ACT.Copy).then_inc(b_rowsb, 1)
            act.wait_ge(b_rowsb, 1)
            act.dma_start(b_scr, brow[:].rearrange("h (o m) -> h o m", o=1).to_broadcast([HEADS, P, ROWLEN])
                          ).then_inc(b_out, 16)
            act.wait_ge(c_in, 144)
            act.wait_ge(xt_a, 4)
            act.wait_ge(xt_d, 4)

            def square(src, f, n):
                if 8 * n + f >= 2:
                    act.wait_ge(sq_added, 8 * n + f - 1)
                nc.scalar.activation(S[:, f % 2, :], src[:, f, :], ACT.Square).then_inc(sq_ready, 1)

            def split_input(src, dst, gain, scr, j, n):
                for f in range(KD):
                    if j:
                        act.wait_ge(x_added, 8 * (j - 1) + f + 1)
                    nc.scalar.activation(dst[:, f, :], src[:, f, :], ACT.Copy, scale=gain[:, f:f + 1]
                                         ).then_inc(xh_ready, 1)
                    square(src, f, n)
                    act.dma_start(scr[f * P:(f + 1) * P, :], src[:, f, :]).then_inc(x_out, 16)
            split_input(XT, XH, g_pre1, x_scr[0], 0, 0)

            for T in range(START["q"], START["gate1"]):
                hi(T + 1)

            def gates(i):
                for t in range(4):
                    T0 = START["gate1"] + t
                    hi_next(T0, 4, i)
                    ev_wait(act, T0, 4, i)
                    if t >= 2 or not first_turn(i):
                        act.wait_ge(g_out[t % 2], plus(16 * (t // 2), 32, i))
                    nc.scalar.activation(gst[:, t % 2, :], S[:, t % 2, :], ACT.Sigmoid).then_inc(g_post, 1)
                    act.wait_ge(g_post, plus(t + 1, 4, i))
                    gd = g_scr.rearrange("(f p) t -> p f t", p=P)
                    act.dma_start(row(gd, plus(t, 4, i)), gst[:, t % 2, :]).then_inc(g_out[t % 2], 16)
            repeat(act, 4, gates)
            for t in range(4):
                if t < 3:
                    hi(START["u"] + t + 1)
                ev_wait(act, START["u"] + t)
                act.dma_start(u_scr[t * P:(t + 1) * P, :], ust[:, t % 2, :]).then_inc(u_out[t % 2], 16)
            units = [(n, g) for n in range(MT) for g in range(KV)]

            def exps(u):
                n, g = units[u]
                lo = P if n == 0 else 0
                act.wait_ge(nm_ready, u + 1)
                c = 4 * (u % 2)
                for j in range(4):
                    nc.scalar.activation(prob[:, u % 2, j, lo:], prob[:, u % 2, j, lo:], ACT.Exp,
                                         bias=nm[:, c + j:c + j + 1], accum_out=den[:, c + j:c + j + 1]
                                         ).then_inc(achain, 1)
                nc.scalar.activation(es[:, c:c + 4], es[:, c:c + 4], ACT.Exp).then_inc(p_ready, 1)
                
            exps(0)
            for u, (n, g) in enumerate(units):
                act.wait_ge(pt_ready, u + 1)
                half = slice(4, 8) if n == 0 else slice(0, 8)
                nc.scalar.activation(probT[:, u % 2, half, :],
                                     aux[0][:].rearrange("p (a t) -> p a t", a=8)[:, half, :], ACT.Copy).then_inc(ptc, 1)
                if u + 1 < len(units):
                    exps(u + 1)
                act.wait_ge(aot_ready, u + 1)
                nc.scalar.activation(AOH[:, 2 * g:2 * g + 2, n * P:(n + 1) * P],
                                     aux[1][:, 512:768].rearrange("p (a t) -> p a t", a=2), ACT.Copy).then_inc(aoh, 1)

            act.wait_ge(par_in, 16 * 17)
            nc.scalar.activation(lam[:, 3, :], lam[:, 2, :], ACT.Exp).then_inc(a1, 1)
            act.wait_ge(a2, 1)
            nc.scalar.activation(lam[:, 5, :], lam[:, 4, :], ACT.Exp).then_inc(a3, 1)
            act.wait_ge(a2, 2)
            nc.scalar.activation(lam[:, 12, :], lam[:, 10, :], ACT.Sin).then_inc(a3, 1)
            nc.scalar.activation(lam[:, 13, :], lam[:, 11, :], ACT.Sin).then_inc(a3, 1)
            for b in range(4):
                act.wait_ge(et_ready, b + 1)
                dst = (ETr, ETi)[b // 2]
                nc.scalar.activation(dst[:, (b % 2) * 8:(b % 2) * 8 + 8, :],
                                     (acc + aux)[b][:].rearrange("p (a t) -> p a t", a=8), ACT.Copy).then_inc(et_copied, 1)
            for h in range(2):
                act.wait_ge(yk_ready, 2 * h + 1)
                nc.scalar.activation(Ysb[:, 16 * h:16 * h + 8, :].rearrange("p (a b) t -> p b a t", b=2),
                                     (acc + aux)[2 * h][:].rearrange("p (b a t) -> p b a t", b=2, a=4),
                                     ACT.Copy).then_inc(y_sb, 1)
            hi(START["glu"])
            act.wait_ge(z_in, 64)
            for t in range(KW):
                nc.scalar.activation(Z[:, t, :], Z[:, t, :], ACT.Gelu_apprx_tanh).then_inc(z_act, 1)
            for t in range(KW):
                act.wait_ge(z_act, t + 1)
                nc.scalar.activation(ZH[:, t, :], Z[:, t, :], ACT.Copy).then_inc(zh_ready, 1)
            for t in range(KW):
                T = START["glu"] + t
                hi(T + 1)
                act.wait_ge(tile_done, T + 1)
                if t >= 2:
                    act.wait_ge(z2l, t - 1)
                nc.scalar.activation(S[:, t % 2, :], acc[T % 2][:], ACT.Sigmoid).then_inc(ev(T), 1)
                act.wait_ge(glu_mul, t + 1)
                nc.scalar.activation(perm(Z2H[:, t, :]), unperm(S[:, t % 2, :]), ACT.Copy).then_inc(z2h, 1)

            def merge1(i):
                for t in range(4):
                    T0 = START["merge1"] + t
                    hi_next(T0, 4, i)
                    if t >= 2:
                        act.wait_ge(m_sum, plus(t - 1, 2, i))
                        nc.scalar.activation(row(MH, plus(t - 2, 2, i)), S[:, t % 2, :], ACT.Copy).then_inc(mh_ready, 1)
            repeat(act, 4, merge1)
            for t in range(8):
                T = START["wout"] + t
                hi(T + 1)
                ev_wait(act, T)
                square(F, t, 1)
            split_input(F, YH, g_pre2, x_scr[1], 1, 2)

            def ff(c):
                for t in range(12):
                    T0 = START["ff"] + t
                    hi_next(T0, 12, c)
                    if t < 4:
                        act.wait_ge(tile_done, plus(T0 + 1, 12, c))
                        if t >= 2 or not first_turn(c):
                            act.wait_ge(hl, plus(t - 1, 4, c))
                        nc.scalar.activation(S[:, t % 2, :], acc[T0 % 2][:], ACT.Relu).then_inc(ev(T0), 1)
                        act.wait_ge(hsq, plus(t + 1, 4, c))
                        nc.scalar.activation(HH[:, t, :], S[:, t % 2, :], ACT.Copy).then_inc(hh, 1)
            act.wait_ge(sq_added, 24)
            repeat(act, FCH, ff)
            for f in range(KD):
                act.wait_ge(f_final, f + 1)
                square(F, f, 3)
            split_input(F, YH, g_pre3, x_scr[2], 2, 4)

            for t in range(4):
                T = START["v2"] + t
                hi(T + 1)
            ev_wait(act, START["v2"] + 2)
            ev_wait(act, START["v2"] + 3)
            for m in range(MT):
                nc.scalar.activation(V2[:, m, :], V2[:, m, :], ACT.Gelu_apprx_tanh).then_inc(v2_gelu, 1)
            act.wait_ge(ws_t, 1)
            nc.scalar.activation(wst[:], aux[0][:].rearrange("p (g t) -> p g t", g=8), ACT.Copy).then_inc(ws_c, 1)
            for t in range(8):
                T = START["au"] + t
                hi(T + 1)
                ev_wait(act, T)
                if t < 4:
                    nc.scalar.activation(Y[:, t, :], S[:, t % 2, :], ACT.Gelu_apprx_tanh).then_inc(uA, 1)
                else:
                    if t >= 6:
                        act.wait_ge(yA, t - 5)
                    nc.scalar.activation(Gb[t % 2][:], S[:, t % 2, :], ACT.Silu).then_inc(uA, 1)
            for t in range(KW):
                act.wait_ge(sg_mul, t + 1)
                nc.scalar.activation(BH[:, t, :], S[:, t % 2, :], ACT.Copy).then_inc(bh, 1)

            def merge2(stage, n):
                def turn(i):
                    for t in range(4):
                        T0 = START[stage] + t
                        hi_next(T0, 4, i)
                        if t < 2:
                            ev_wait(act, T0, 4, i)
                            nc.scalar.activation(Gb[t][:], S[:, t, :], ACT.Sigmoid).then_inc(mg_g, 1)
                repeat(act, 4, turn)
            merge2("amerge", 0)
            for t in range(16):
                T = START["bx"] + t
                hi(T + 1)
                if t >= 12:
                    j = t - 12
                    ev_wait(act, T)
                    nc.scalar.activation(Gb[j % 2][:], S[:, j % 2, :], ACT.Silu).then_inc(b6, 1)
                    act.wait_ge(b4, j + 1)
                    nc.scalar.activation(BH[:, j, :], Y[:, j, :], ACT.Copy).then_inc(bh, 1)
            merge2("bmerge", 1)
            for t in range(12):
                T = START["cx"] + t
                hi(T + 1)
                if t < 4:
                    act.wait_ge(c1, t + 1)
                    nc.scalar.activation(BH[:, t, :], Gb[t % 2][:], ACT.Copy).then_inc(bh, 1)
                elif t < 8:
                    ev_wait(act, T)
                    nc.scalar.activation(Y[:, t - 4, :], S[:, t % 2, :], ACT.Silu).then_inc(c2, 1)
                else:
                    ev_wait(act, T)
                    nc.scalar.activation(BH[:, t - 8, :], S[:, t % 2, :], ACT.Copy).then_inc(bh, 1)
            merge2("cmerge", 2)
            for i in range(4):
                p0 = NT // 2 + i
                act.wait_ge(w_in_s[p0 % 2], 16 * (4 + p0 // 2))
                if i == 0:
                    act.wait_ge(tile_done, NT)
                nc.scalar.activation(WOH[:, :, 256 * i:256 * (i + 1)], raw[:, p0 % 2], ACT.Copy).then_inc(wo_hi, 1)
                for f in (2 * i, 2 * i + 1):
                    act.wait_ge(mg_m, 24)
                    nc.scalar.activation(NH[:, f, :], M[:, f, :], ACT.Copy).then_inc(nh, 1)
            for m in range(MT):
                act.wait_ge(ot_ready, m + 1)
                if m >= 1:
                    act.wait_ge(fsum, m)
                nc.scalar.activation(Gb[0][:], acc[m % 2][:], ACT.Square, accum_out=ss[:, m:m + 1]).then_inc(fsum, 1)

        @block.vector
        def _(dve):
            chain = [0]

            def link(ins):
                chain[0] += 1
                ins.then_inc(dchain, 1)
                dve.wait_ge(dchain, chain[0])

            TT, TS, STT = nc.vector.tensor_tensor, nc.vector.tensor_scalar, nc.vector.scalar_tensor_tensor

            def lo(T0, per=0, i=0):
                if T0 >= NT:
                    return
                dve.wait_ge(w_hi, plus(T0 + 1, per, i))
                kb = KOF[T0]
                TT(WL[:, T0 % 2, 0:kb, :], raw[:, (T0 // 2) % 2, 0:kb, (T0 % 2) * P:(T0 % 2 + 1) * P],
                   WH[:, T0 % 2, 0:kb, :].bitcast(f32), ALU.subtract).then_inc(w_lo, 1)

            def lo_next(T0, per, i):
                lo(T0 + 1 + per * i) if isinstance(i, int) else lo(T0 + 1, per, i)

            def done(T0, per=0, i=0):
                dve.wait_ge(tile_done, plus(T0 + 1, per, i))

            nc.vector.memset(one_col, 1.0 / D).then_inc(const_set, 1)
            nc.vector.memset(half_neg, -0.5).then_inc(const_set, 1)
            nc.vector.memset(ones[:], 1.0).then_inc(const_set, 1)
            for m in range(1, MT, 2):
                dve.wait_ge(xt_ready, m + 1)
                nc.vector.tensor_copy(XT[:, :, m * P:(m + 1) * P],
                                      aux[1][:].rearrange("p (k t) -> p k t", k=KD)).then_inc(xt_d, 1)
            lo(0)
            dve.wait_ge(c_in, 144)
            dve.wait_ge(id_in, 16)
            dve.wait_ge(xt_a, 4)
            dve.wait_ge(xt_d, 4)

            def split_tile(src, dh, dl, gain, f, j):
                dve.wait_ge(xh_ready, 8 * j + f + 1)
                STT(dl[:, f, :], src[:, f, :], gain[:, f:f + 1], dh[:, f, :].bitcast(f32), ALU.mult, ALU.subtract
                    ).then_inc(xl_ready, 1)

            def rms(n, dst):
                dve.wait_ge(mean_ready, n + 1)
                TS(ms, aux[0][:, 0:KD], RMS_EPS, None, ALU.add).then_inc(ms_ready, 1)
                dve.wait_ge(rtok_ready, n + 1)
                TT(ACC[:].rearrange("p (a b) -> p a b", a=MT), ident[:].rearrange("p (o b) -> p o b", o=1).to_broadcast([P, MT, P]),
                   rtok.rearrange("p (a o) -> p a o", o=1).to_broadcast([P, MT, P]), ALU.mult).then_inc(rdg_ready, 1)
                dve.wait_ge(rb_ready, n + 1)
                link(nc.vector.tensor_copy(dst[:], aux[1][:]))

            for f in range(KD):
                split_tile(XT, XH, XL, g_pre1, f, 0)
            rms(0, RA)
            dve.wait_ge(x_out, 16 * 8)
            dve.wait_ge(sq_added, 8)
            dve.wait_ge(xl_ready, 8)
            for T in range(START["q"], START["gate1"]):
                lo(T + 1)
                done(T)
                if T < 5:
                    TT(q[:, T, :] if T < 4 else k_[:], acc[T % 2][:], RA[:], ALU.mult).then_inc(ev(T), 1)
                else:
                    TT(v[:], acc[T % 2][:].rearrange("p (m n) -> p m n", m=MT),
                       rtok.rearrange("p (a o) -> p a o", o=1).to_broadcast([P, MT, P]), ALU.mult
                       ).then_inc(ev(T), 1)

            def gates(i):
                for t in range(4):
                    T0 = START["gate1"] + t
                    lo_next(T0, 4, i)
                    done(T0, 4, i)
                    if t >= 2 or not first_turn(i):
                        dve.wait_ge(g_post, plus(t - 1, 4, i))
                    TT(S[:, t % 2, :], acc[T0 % 2][:], RA[:], ALU.mult).then_inc(ev(T0), 1)
            repeat(dve, 4, gates)
            for t in range(4):
                T = START["u"] + t
                if t < 3:
                    lo(T + 1)
                done(T)
                if t >= 2:
                    dve.wait_ge(u_out[t % 2], 16)
                TT(unperm(ust[:, t % 2, :]), perm(acc[T % 2][:]), perm(RA[:]), ALU.mult).then_inc(ev(T), 1)

            units = [(n, g) for n in range(MT) for g in range(KV)]
            dve.wait_ge(b_in, 16)
            dve.wait_ge(g_post, 16)

            def soft(u):
                n, g = units[u]
                lo_ = P if n == 0 else 0
                c = 4 * (u % 2)
                dve.wait_ge(s_ready, u + 1)
                if u >= 2:
                    dve.wait_ge(pt_ready, u - 1)
                L = prob[:, u % 2, :, lo_:]
                STT(L, acc[u % 2][:].rearrange("p (j s) -> p j s", j=4)[:, :, lo_:], HD ** -0.5,
                    bias[:, 4 * g:4 * g + 4, lo_:], ALU.mult, ALU.add).then_inc(s_read, 1)
                dve.wait_ge(s_read, u + 1)
                link(nc.vector.reduce_max(mx[:, c:c + 4], L, AX.X))
                link(TT(mx[:, c:c + 4], mx[:, c:c + 4], sink[:, 4 * g:4 * g + 4], ALU.max))
                link(TS(nm[:, c:c + 4], mx[:, c:c + 4], -1.0, None, ALU.mult))
                TT(es[:, c:c + 4], sink[:, 4 * g:4 * g + 4], mx[:, c:c + 4], ALU.subtract).then_inc(nm_ready, 1)
            soft(0)
            for u, (n, g) in enumerate(units):
                if u + 1 < len(units):
                    soft(u + 1)
                c = 4 * (u % 2)
                dve.wait_ge(p_ready, u + 1)
                link(TT(den[:, c:c + 4], den[:, c:c + 4], es[:, c:c + 4], ALU.add))
                link(nc.vector.reciprocal(rd[:, c:c + 4], den[:, c:c + 4]))
                dve.wait_ge(o_ready, u + 1)
                if u >= 2:
                    dve.wait_ge(aot_ready, u - 1)
                TT(otok[:, u % 2, :].rearrange("p (j d) -> p j d", j=4), aux[1][:, 0:256].rearrange("p (j d) -> p j d", j=4),
                   rd[:, c:c + 4].rearrange("p (j o) -> p j o", o=1).to_broadcast([P, 4, HD]), ALU.mult).then_inc(o_read, 1)
                dve.wait_ge(aoh, u + 1)
                sl = (slice(None), slice(2 * g, 2 * g + 2), slice(n * P, (n + 1) * P))
                TT(AOL[sl], aux[1][:, 512:768].rearrange("p (a t) -> p a t", a=2), AOH[sl].bitcast(f32), ALU.subtract
                   ).then_inc(aot_read, 1)

            LR, LI, DT, ZR, MAG, PHI = (lam[:, n, :] for n in (0, 1, 3, 4, 5, 6))
            T1, T2, T3, RED, REDC, SN, CS = (lam[:, n, :] for n in (7, 8, 9, 10, 11, 12, 13))
            AR, AI = lam[:, 14, :], lam[:, 15, :]
            FR, FI, NRR, RHO = lam[:, 16, :], lam[:, 17, :], lam[:, 18, :], lam[:, 19, :]
            dve.wait_ge(a1, 1)
            TT(ZR, LR, DT, ALU.mult).then_inc(a2, 1)
            link(TT(PHI, LI, DT, ALU.mult))
            TWO_PI = 2 * np.pi
            P1 = 6.28125
            P2 = float(np.float32(round((TWO_PI - P1) * 2 ** 20) / 2 ** 20))
            P3 = float(TWO_PI - P1 - P2)
            ROUND = 1.5 * 2 ** 23
            link(TS(T1, PHI, float(1 / TWO_PI), None, ALU.mult))
            link(TS(T1, T1, ROUND, None, ALU.add))
            link(TS(T1, T1, ROUND, None, ALU.subtract))
            link(STT(T2, T1, -P1, PHI, ALU.mult, ALU.add))
            link(STT(T2, T1, -P2, T2, ALU.mult, ALU.add))
            link(STT(T2, T1, -P3, T2, ALU.mult, ALU.add))
            PI = float(np.nextafter(np.float32(np.pi), np.float32(0)))
            link(TS(RED, T2, PI, -PI, ALU.min, ALU.max))
            link(TS(T3, RED, -1.0, None, ALU.mult))
            link(TT(T3, T3, RED, ALU.max))
            TS(REDC, T3, -1.0, float(np.pi / 2), ALU.mult, ALU.add).then_inc(a2, 1)
            dve.wait_ge(a3, 3)
            def unit(cr, ci):
                link(TT(T1, cr, cr, ALU.mult))
                link(TT(T2, ci, ci, ALU.mult))
                link(TT(T1, T1, T2, ALU.add))
                link(TS(T1, T1, -0.5, 1.5, ALU.mult, ALU.add))
                link(TT(cr, cr, T1, ALU.mult))
                link(TT(ci, ci, T1, ALU.mult))
            unit(CS, SN)
            link(TT(AR, MAG, CS, ALU.mult))
            link(TT(AI, MAG, SN, ALU.mult))
            link(TS(NRR, AR, -1.0, None, ALU.add))
            link(TT(T1, LR, LR, ALU.mult))
            link(TT(T2, LI, LI, ALU.mult))
            link(TT(T1, T1, T2, ALU.add))
            link(nc.vector.reciprocal(T3, T1))
            link(TT(T1, NRR, LR, ALU.mult))
            link(TT(T2, AI, LI, ALU.mult))
            link(TT(T1, T1, T2, ALU.add))
            link(TT(FR, T1, T3, ALU.mult))
            link(TT(T1, AI, LR, ALU.mult))
            link(TT(T2, NRR, LI, ALU.mult))
            link(TT(T1, T1, T2, ALU.subtract))
            link(TT(FI, T1, T3, ALU.mult))

            def cmul(dr, di, ar, ai, br, bi, t1, t2):
                link(TT(t1, ar, br, ALU.mult))
                link(TT(t2, ai, bi, ALU.mult))
                link(TT(t1, t1, t2, ALU.subtract))
                link(TT(t2, ar, bi, ALU.mult))
                link(TT(di, ai, br, ALU.mult))
                link(TT(di, di, t2, ALU.add))
                link(nc.vector.tensor_copy(dr, t1))

            def over_c(a):
                return a.rearrange("p (a o) -> p a o", o=1).to_broadcast([P, PAIRS, C])
            c1_, c2_ = (ct[:, n, :].rearrange("p (a c) -> p a c", c=C) for n in (0, 1))
            cmul(Bbr[:], Bbi[:], Br[:], Bi[:], over_c(FR), over_c(FI), c1_, c2_)
            link(nc.vector.memset(Ar[:, 0, :], 1.0))
            link(nc.vector.memset(Ai[:, 0, :], 0.0))
            link(nc.vector.tensor_copy(Ar[:, 1, :], AR))
            link(nc.vector.tensor_copy(Ai[:, 1, :], AI))
            for n in range(2, TAU + 1):
                a, b = (n // 2, n - n // 2)
                cmul(Ar[:, n, :], Ai[:, n, :], Ar[:, a, :], Ai[:, a, :], Ar[:, b, :], Ai[:, b, :], T1, T2)
            for n in range(2):
                for t in range(4):
                    dve.wait_ge(ct_ready, 4 * n + 4)
                    src = aux[n][:].rearrange("p (t a b c) -> p t a b c", t=8, a=4, b=2)
                    dst = (Cr, Ci)[n]
                    for g2 in range(2):
                        pp = slice(g2 * NS, (g2 + 1) * NS)
                        link(nc.vector.tensor_copy(dst[pp, 4 * t:4 * t + 4, :], src[pp, t, :, g2, :]))
            for n in range(TAU + 1):
                ar, ai = over_c(Ar[:, n, :]), over_c(Ai[:, n, :])
                link(TT(c1_, Cr[:], ar, ALU.mult))
                link(TT(c2_, Ci[:], ai, ALU.mult))
                link(TT(FXr[:, :, n, :], c1_, c2_, ALU.subtract))
                link(TT(c1_, Ci[:], ar, ALU.mult))
                link(TT(c2_, Cr[:], ai, ALU.mult))
                link(STT(FXi[:, :, n, :], c1_, -1.0, c2_, ALU.mult, ALU.subtract))
            for src, dst in ((Bbr, BBr), (Bbi, BBi)):
                link(nc.vector.memset(dst[:], 0.0))
                for g2 in range(2):
                    pp = slice(g2 * NS, (g2 + 1) * NS)
                    link(nc.vector.tensor_copy(dst[pp, :, g2, :], src[pp]))
            for t in range(TAU):
                n = TAU - 1 - t
                ar, ai = over_c(Ar[:, n, :]), over_c(Ai[:, n, :])
                link(TT(c1_, Bbr[:], ar, ALU.mult))
                link(TT(c2_, Bbi[:], ai, ALU.mult))
                link(TT(M1r[:, :, t, :], c1_, c2_, ALU.subtract))
                link(TT(c1_, Bbi[:], ar, ALU.mult))
                link(TT(c2_, Bbr[:], ai, ALU.mult))
                link(TT(M1i[:, :, t, :], c1_, c2_, ALU.add))
            nc.vector.tensor_copy(lam[:, 20, :], CS).then_inc(m1_ready, 1)
            dve.wait_ge(k_ready, 1)
            for h in range(2):
                link(nc.vector.tensor_copy(Kt[:, 8 * h:8 * h + 8, :],
                                           acc[h][0:32, :].rearrange("p (a m) -> p a m", a=8)))
            kd = ct[0:32, 0, :].rearrange("p (a c) -> p a c", c=C)
            link(TT(kd, dsk[:].rearrange("p (a o) -> p a o", o=1).to_broadcast([32, PAIRS, C]),
                    eye16[:].rearrange("p (o c) -> p o c", o=1).to_broadcast([32, PAIRS, C]), ALU.mult))
            TT(Kt[:, :, 0:C], Kt[:, :, 0:C], kd, ALU.add).then_inc(k_copied, 1)
            for _n in range(3):
                cmul(CS, SN, CS, SN, CS, SN, T1, T2)
            unit(CS, SN)
            dve.wait_ge(et_copied, 4)
            link(nc.vector.memset(RC[:, :, 0:1], 1.0))
            link(nc.vector.memset(RS[:, :, 0:1], 0.0))
            m = 1
            while m < CH:
                t1 = rt[:, 0, 0:PAIRS * m].rearrange("p (a m) -> p a m", m=m)
                t2 = rt[:, 1, 0:PAIRS * m].rearrange("p (a m) -> p a m", m=m)
                wr = CS.rearrange("p (a o) -> p a o", o=1).to_broadcast([P, PAIRS, m])
                wi = SN.rearrange("p (a o) -> p a o", o=1).to_broadcast([P, PAIRS, m])
                cmul(RC[:, :, m:2 * m], RS[:, :, m:2 * m], RC[:, :, 0:m], RS[:, :, 0:m], wr, wi, t1, t2)
                m *= 2
                if m < CH:
                    cmul(CS, SN, CS, SN, CS, SN, T1, T2)
                    unit(CS, SN)
            link(TT(RHO, MAG, MAG, ALU.mult))
            link(TT(RHO, RHO, RHO, ALU.mult))
            link(TT(RHO, RHO, RHO, ALU.mult))
            dve.wait_ge(l_in, 16 * 16)
            link(nc.vector.tensor_copy(Dk[:], RHO.rearrange("p (a o) -> p a o", o=1).to_broadcast([P, PAIRS, CH])))
            link(nc.vector.memset(Dk[:, :, 0:1], 0.0))
            flat = lambda t: t[:].rearrange("p a h -> p (a h)")
            for h in range(2):
                sl = slice(1024 * h, 1024 * (h + 1))
                dve.wait_ge(x_ready, h + 1)
                xr_, xi_ = acc[h][:], aux[h][:]
                link(TT(S[:, 0, :], xr_, flat(RC)[:, sl], ALU.mult))
                link(TT(S[:, 1, :], xi_, flat(RS)[:, sl], ALU.mult))
                link(TT(flat(Vr)[:, sl], S[:, 0, :], S[:, 1, :], ALU.add))
                link(TT(S[:, 0, :], xi_, flat(RC)[:, sl], ALU.mult))
                link(TT(S[:, 1, :], xr_, flat(RS)[:, sl], ALU.mult))
                link(TT(flat(Vi)[:, sl], S[:, 0, :], S[:, 1, :], ALU.subtract))
            for t in (Vr, Vi):
                link(nc.vector.tensor_tensor_scan(flat(t), flat(Dk), flat(t), 0.0, ALU.mult, ALU.add))
            a, b = slice(1, CH), slice(0, CH - 1)
            link(nc.vector.memset(Hr[:, :, 0:1], 0.0))
            link(nc.vector.memset(Hi[:, :, 0:1], 0.0))
            link(TT(Hr[:, :, a], Vr[:, :, b], RC[:, :, b], ALU.mult))
            link(TT(Dk[:, :, b], Vi[:, :, b], RS[:, :, b], ALU.mult))
            link(TT(Hr[:, :, a], Hr[:, :, a], Dk[:, :, b], ALU.subtract))
            link(TT(Hi[:, :, a], Vr[:, :, b], RS[:, :, b], ALU.mult))
            link(TT(Dk[:, :, b], Vi[:, :, b], RC[:, :, b], ALU.mult))
            TT(Hi[:, :, a], Hi[:, :, a], Dk[:, :, b], ALU.add).then_inc(h_ready, 1)
            for h in range(2):
                dve.wait_ge(yk_ready, 2 * h + 2)
                nc.vector.tensor_copy(Ysb[:, 16 * h + 8:16 * h + 16, :].rearrange("p (a b) t -> p b a t", b=2),
                                      (acc + aux)[2 * h + 1][:].rearrange("p (b a t) -> p b a t", b=2, a=4)
                                      ).then_inc(y_sb, 1)
            lo(START["glu"])
            for t in range(KW):
                dve.wait_ge(zh_ready, t + 1)
                TT(ZL[:, t, :], Z[:, t, :], ZH[:, t, :].bitcast(f32), ALU.subtract).then_inc(zl_ready, 1)
            for t in range(KW):
                T = START["glu"] + t
                lo(T + 1)
                ev_wait(dve, T)
                TT(S[:, t % 2, :], S[:, t % 2, :], Z[:, t, :], ALU.mult).then_inc(glu_mul, 1)
                dve.wait_ge(z2h, t + 1)
                TT(perm(Z2L[:, t, :]), unperm(S[:, t % 2, :]), perm(Z2H[:, t, :]).bitcast(f32), ALU.subtract
                   ).then_inc(z2l, 1)
            dve.wait_ge(z2l, 4)

            def merge1(i):
                for t in range(4):
                    T0 = START["merge1"] + t
                    lo_next(T0, 4, i)
                    done(T0, 4, i)
                    dve.wait_ge(ga_in[t], plus(16, 16, i))
                    if t < 2:
                        if not first_turn(i):
                            dve.wait_ge(ml_ready, plus(t - 1, 2, i))
                        TT(S[:, t, :], acc[T0 % 2][:], gin[:, t, :], ALU.mult).then_inc(ev(T0), 1)
                    else:
                        if not first_turn(i):
                            dve.wait_ge(m_sum, plus(t - 3, 2, i))
                        gt = (ACC, RP)[t % 2]
                        TT(gt[:], acc[T0 % 2][:], gin[:, t, :], ALU.mult).then_inc(ev(T0), 1)
                        ev_wait(dve, T0, 4, i)
                        ev_wait(dve, T0 - 2, 4, i)
                        TT(S[:, t % 2, :], S[:, t % 2, :], gt[:], ALU.add).then_inc(m_sum, 1)
                        dve.wait_ge(mh_ready, plus(t - 1, 2, i))
                        f = plus(t - 2, 2, i)
                        TT(row(ML, f), S[:, t % 2, :], row(MH, f).bitcast(f32), ALU.subtract).then_inc(ml_ready, 1)
            repeat(dve, 4, merge1)
            for t in range(8):
                T = START["wout"] + t
                lo(T + 1)
                done(T)
                nc.vector.tensor_copy(F[:, t, :], acc[T % 2][:]).then_inc(ev(T), 1)

            def post_norm(n, j, gpost, gpre):
                rms(n, RP)
                for f in range(KD + 1):
                    if f < KD:
                        STT(F[:, f, :], F[:, f, :], gpost[:, f:f + 1], RP[:], ALU.mult, ALU.mult).then_inc(f_scaled, 1)
                    if f >= 1:
                        split_tile(F, YH, YL, gpre, f - 1, j)
            ev_wait(dve, START["wout"] + 6)
            ev_wait(dve, START["wout"] + 7)
            post_norm(1, 1, g_post1, g_pre2)
            rms(2, RA)
            link(TT(RA[:], RA[:], RA[:], ALU.mult))

            def ff(c):
                for t in range(12):
                    T0 = START["ff"] + t
                    lo_next(T0, 12, c)
                    done(T0, 12, c)
                    if t < 4:
                        ev_wait(dve, T0, 12, c)
                        TT(S[:, t % 2, :], S[:, t % 2, :], S[:, t % 2, :], ALU.mult).then_inc(hsq, 1)
                        dve.wait_ge(hh, plus(t + 1, 4, c))
                        TT(HL[:, t, :], S[:, t % 2, :], HH[:, t, :].bitcast(f32), ALU.subtract).then_inc(hl, 1)
                    else:
                        f = t - 4
                        if first_turn(c):
                            dve.wait_ge(f_zero, 1)
                        ev_wait(dve, T0 - 12, 12, c)
                        TT(F[:, f, :], F[:, f, :], acc[T0 % 2][:], ALU.add).then_inc(ev(T0), 1)
                        if isinstance(c, int) and c == FCH - 1:
                            ev_wait(dve, T0, 12, c)
                            TT(F[:, f, :], F[:, f, :], RA[:], ALU.mult).then_inc(f_final, 1)
            repeat(dve, FCH, ff)
            dve.wait_ge(f_final, 8)
            post_norm(3, 2, g_post2, g_pre3)
            rms(4, RA)

            dve.wait_ge(xl_ready, 24)
            dve.wait_ge(x_out, 16 * 24)
            dve.wait_ge(sq_added, 40)
            for t in range(4):
                T = START["v2"] + t
                lo(T + 1)
                done(T)
                TT(V2[:, :, t * P:(t + 1) * P], acc[T % 2][:].rearrange("p (m n) -> p m n", m=MT),
                   rtok.rearrange("p (a o) -> p a o", o=1).to_broadcast([P, MT, P]), ALU.mult).then_inc(ev(T), 1)
            dve.wait_ge(p2_in, 16 * 6)
            for t in range(8):
                T = START["au"] + t
                lo(T + 1)
                vt = V2[:, t, :]
                dve.wait_ge(v2_gelu, t + 1)
                link(nc.vector.bn_stats(bn, vt))
                link(nc.vector.bn_aggr(ag, bn))
                TS(lnv, ag[:, 1:2], LN_EPS, None, ALU.add).then_inc(ln_var, 1)
                dve.wait_ge(ln_r, t + 1)
                link(TS(vt, vt, ag[:, 0:1], lnr, ALU.subtract, ALU.mult))
                link(TT(vt, vt, lng[:], ALU.mult))
                TT(vt, vt, lnb[:], ALU.add).then_inc(ln_done, 1)
                done(T)
                if t >= 2:
                    dve.wait_ge(uA, t - 1)
                TT(S[:, t % 2, :], acc[T % 2][:], RA[:], ALU.mult).then_inc(ev(T), 1)
                if t >= 4:
                    dve.wait_ge(uA, t + 1)
                    TT(Y[:, t - 4, :], Y[:, t - 4, :], Gb[t % 2][:], ALU.mult).then_inc(yA, 1)
            for t in range(KW):
                dve.wait_ge(sg_ready, t + 1)
                dve.wait_ge(uA, 8)
                if t >= 2:
                    dve.wait_ge(bl, t - 1)
                TT(S[:, t % 2, :].rearrange("p (n t) -> p n t", n=MT), aux[t % 2][:].rearrange("p (n t) -> p n t", n=MT),
                   bsb[:, t:t + 1, :].to_broadcast([P, MT, P]), ALU.add).then_inc(sg_add, 1)
                dve.wait_ge(sg_add, t + 1)
                dve.wait_ge(yA, t + 1)
                TT(S[:, t % 2, :], S[:, t % 2, :], Y[:, t, :], ALU.mult).then_inc(sg_mul, 1)
                dve.wait_ge(bh, t + 1)
                TT(BL[:, t, :], S[:, t % 2, :], BH[:, t, :].bitcast(f32), ALU.subtract).then_inc(bl, 1)

            def merge2(stage, n):
                def turn(i):
                    for t in range(4):
                        T0 = START[stage] + t
                        lo_next(T0, 4, i)
                        done(T0, 4, i)
                        if t < 2:
                            if not first_turn(i):
                                dve.wait_ge(mg_m, plus(8 * n + t - 1, 2, i))
                            TT(S[:, t, :], acc[T0 % 2][:], RA[:], ALU.mult).then_inc(ev(T0), 1)
                        else:
                            dve.wait_ge(mg_g, plus(8 * n + t - 1, 2, i))
                            TT(S[:, t % 2, :], acc[T0 % 2][:], Gb[t % 2][:], ALU.mult).then_inc(ev(T0), 1)
                repeat(dve, 4, turn)
                dve.wait_ge(mg_m, 8 * (n + 1))
            dve.wait_ge(bl, 4)
            merge2("amerge", 0)
            for t in range(16):
                T = START["bx"] + t
                j = t % 4
                lo(T + 1)
                done(T)
                if t < 4:
                    TT(Y[:, j, :], acc[T % 2][:], RA[:], ALU.mult).then_inc(ev(T), 1)
                elif t < 8:
                    Gj, Yj = Gb[j % 2], Y[:, j, :]
                    if j >= 2:
                        dve.wait_ge(b3, j - 1)
                    ev_wait(dve, START["bx"] + j)
                    TT(Gj[:], acc[T % 2][:], RA[:], ALU.mult).then_inc(ev(T), 1)
                    ev_wait(dve, T)
                    link(TT(Gj[:], Gj[:], Yj, ALU.mult))
                    link(TS(Yj, Gj[:], cw[:, 2 * KW + j:2 * KW + j + 1], cb[:, j:j + 1], ALU.mult, ALU.add))
                    link(STT(Yj[:, 1:], Gj[:, :SEQ - 1], cw[:, KW + j:KW + j + 1], Yj[:, 1:], ALU.mult, ALU.add))
                    STT(Yj[:, 2:], Gj[:, :SEQ - 2], cw[:, j:j + 1], Yj[:, 2:], ALU.mult, ALU.add).then_inc(b3, 1)
                elif t < 12:
                    dve.wait_ge(b3, j + 1)
                    if j >= 2:
                        dve.wait_ge(b2, j - 1)
                    TT(S[:, j % 2, :], acc[T % 2][:], RA[:], ALU.mult).then_inc(ev(T), 1)
                    ev_wait(dve, T)
                    TT(Y[:, j, :], Y[:, j, :], S[:, j % 2, :], ALU.mult).then_inc(b2, 1)
                else:
                    dve.wait_ge(b2, 4)
                    if j >= 2:
                        dve.wait_ge(b6, j - 1)
                    TT(S[:, j % 2, :], acc[T % 2][:], RA[:], ALU.mult).then_inc(ev(T), 1)
                    dve.wait_ge(b6, j + 1)
                    TT(Y[:, j, :], Y[:, j, :], Gb[j % 2][:], ALU.mult).then_inc(b4, 1)
                    dve.wait_ge(bh, 4 + j + 1)
                    TT(BL[:, j, :], Y[:, j, :], BH[:, j, :].bitcast(f32), ALU.subtract).then_inc(bl, 1)
            merge2("bmerge", 1)
            for t in range(12):
                T = START["cx"] + t
                j = t % 4
                lo(T + 1)
                done(T)
                if t < 4:
                    w = POOLS[j]
                    X0 = Y[:, j, :]
                    TT(X0, acc[T % 2][:], RA[:], ALU.mult).then_inc(ev(T), 1)
                    ev_wait(dve, T)
                    if t >= 1:
                        dve.wait_ge(bl, 8 + t)
                    if t == 0:
                        dve.wait_ge(bl, 8)
                    src, shift, n = X0, 1, 0
                    while shift < w:
                        dst = S[:, n % 2, :]
                        link(TT(dst[:, shift:], src[:, shift:], src[:, :SEQ - shift], ALU.add))
                        link(nc.vector.tensor_copy(dst[:, :shift], src[:, :shift]))
                        src, shift, n = dst, 2 * shift, n + 1
                    link(TT(src[:, 0:16], src[:, 0:16], cnt[:, j, :], ALU.mult))
                    STT(Gb[j % 2][:], src, 1.0 / w, X0, ALU.mult, ALU.subtract).then_inc(c1, 1)
                    dve.wait_ge(bh, 8 + j + 1)
                    TT(BL[:, j, :], Gb[j % 2][:], BH[:, j, :].bitcast(f32), ALU.subtract).then_inc(bl, 1)
                elif t < 8:
                    if t == 4:
                        dve.wait_ge(bl, 12)
                    if j >= 2:
                        dve.wait_ge(c2, j - 1)
                    TT(S[:, t % 2, :], acc[T % 2][:], RA[:], ALU.mult).then_inc(ev(T), 1)
                else:
                    dve.wait_ge(c2, 4)
                    if j >= 2:
                        dve.wait_ge(bl, 12 + j - 1)
                    STT(S[:, t % 2, :], acc[T % 2][:], psc[:, j:j + 1], Y[:, j, :], ALU.mult, ALU.mult).then_inc(ev(T), 1)
                    dve.wait_ge(bh, 12 + j + 1)
                    TT(BL[:, j, :], S[:, t % 2, :], BH[:, j, :].bitcast(f32), ALU.subtract).then_inc(bl, 1)
            dve.wait_ge(bl, 16)
            merge2("cmerge", 2)
            for i in range(4):
                p0 = NT // 2 + i
                dve.wait_ge(wo_hi, i + 1)
                TT(WOL[:, :, 256 * i:256 * (i + 1)], raw[:, p0 % 2],
                   WOH[:, :, 256 * i:256 * (i + 1)].bitcast(f32), ALU.subtract).then_inc(wo_lo, 1)
                for f in (2 * i, 2 * i + 1):
                    dve.wait_ge(nh, f + 1)
                    TT(NL[:, f, :], M[:, f, :], NH[:, f, :].bitcast(f32), ALU.subtract).then_inc(nl, 1)
            dve.wait_ge(p_in, 16)
            for m in range(MT):
                dve.wait_ge(fsum, m + 1)
                TS(fv[:, m:m + 1], ss[:, m:m + 1], 1.0 / D, RMS_EPS, ALU.mult, ALU.add).then_inc(fv_r, 1)
                dve.wait_ge(fr_r, m + 1)
                if m >= 2:
                    dve.wait_ge(stored[m % 2], 16 * (m // 2))
                STT(S[:, m % 2, :], acc[m % 2][:], fr[:, m:m + 1], fgb[:], ALU.mult, ALU.mult).then_inc(o_done, 1)

        @block.tensor
        def _(pe):
            mm = nc.tensor.matmul

            def begin(T0, per, i):
                pe.wait_ge(w_lo, plus(T0 + 1, per, i))
                if T0 >= 2:
                    pe.wait_ge(evicted[T0 % 2], plus(T0 // 2, per // 2, i))

            def w_tile(T0, xh, xl, per=0, i=0, each=None):
                begin(T0, per, i)
                kb, a, s_ = KOF[T0], acc[T0 % 2], T0 % 2
                for k in range(kb):
                    if each:
                        each(k)
                    for w, x in ((WH, xh), (WH, xl), (WL, xh)):
                        for h in range(2):
                            sl = slice(512 * h, 512 * (h + 1))
                            last = mm(a[:, sl], w[:, s_, k, :], x[:, k, sl], start=(k == 0 and w is WH and x is xh),
                                      stop=(k == kb - 1 and w is WL))
                last.then_inc(tile_done, 1)

            def token_tile(T0, xh, xl):
                begin(T0, 0, 0)
                a, s_ = acc[T0 % 2], T0 % 2
                for m in range(MT):
                    sl = slice(m * P, (m + 1) * P)
                    for k in range(KD):
                        for w, x in ((WH, xh), (WH, xl), (WL, xh)):
                            last = mm(a[:, sl], x[:, k, sl], w[:, s_, k, :], start=(k == 0 and w is WH and x is xh),
                                      stop=(k == KD - 1 and w is WL))
                last.then_inc(tile_done, 1)

            def norm(n):
                pe.wait_ge(sq_added, 8 * (n + 1))
                for m in range(MT):
                    last = mm(aux[0][:, m:m + 1], ACC[:, m * P:(m + 1) * P], one_col, start=True, stop=True)
                last.then_inc(mean_ready, 1)
                pe.wait_ge(rdg_ready, n + 1)
                for h in range(2):
                    sl = slice(512 * h, 512 * (h + 1))
                    last = mm(aux[1][:, sl], ones[:], ACC[:, sl], start=True, stop=True)
                last.then_inc(rb_ready, 1)

            pe.wait_ge(id_in, 16)
            for m in range(MT):
                pe.wait_ge(x_in[m], 16)
                if m >= 2:
                    pe.wait_ge((xt_a, xt_d)[m % 2], m // 2)
                for k in range(KD):
                    last = nc.tensor.transpose(aux[m % 2][:, k * P:(k + 1) * P], xtok[:, m, k * P:(k + 1) * P], ident[:])
                last.then_inc(xt_ready, 1)
            pe.wait_ge(bs_in, 32)
            pe.wait_ge(ones_set, 1)
            pe.wait_ge(xt_d, 4)
            mm(aux[1][0:HEADS, 0:ROWLEN], rel[:], bsel[:], start=True, stop=True).then_inc(b_row, 1)
            pe.wait_ge(const_set, 3)
            pe.wait_ge(b_rowsb, 1)
            pe.wait_ge(xt_a, 4)
            norm(0)
            w_tile(0, XH, XL, each=lambda k: pe.wait_ge(xl_ready, k + 1))
            for T in range(1, START["gate1"]):
                token_tile(T, XH, XL) if T == 5 else w_tile(T, XH, XL)

            def gates(i):
                for t in range(4):
                    w_tile(START["gate1"] + t, XH, XL, 4, i)
            repeat(pe, 4, gates)
            for t in range(4):
                w_tile(START["u"] + t, XH, XL)

            units = [(n, g) for n in range(MT) for g in range(KV)]
            ev_wait(pe, START["u"] + 2)
            ev_wait(pe, START["u"] + 3)

            def scores(u):
                n, g = units[u]
                lo_ = P if n == 0 else 0
                if u >= 2:
                    pe.wait_ge(s_read, u - 1)
                hp = slice(g * HD, (g + 1) * HD)
                for j in range(4):
                    last = mm(acc[u % 2][:, j * 256 + lo_:(j + 1) * 256], q[hp, j, n * P:(n + 1) * P],
                              k_[hp, (n - 1) * P + lo_:(n + 1) * P], start=True, stop=True)
                last.then_inc(s_ready, 1)
            scores(0)
            for u, (n, g) in enumerate(units):
                if u + 1 < len(units):
                    scores(u + 1)
                pe.wait_ge(p_ready, u + 1)
                if u >= 1:
                    pe.wait_ge(ptc, u)
                halves = (1,) if n == 0 else (0, 1)
                for h in halves:
                    for j in range(4):
                        b = (4 * h + j) * P
                        last = nc.tensor.transpose(aux[0][:, b:b + P], prob[:, u % 2, j, h * P:(h + 1) * P], ident[:])
                last.then_inc(pt_ready, 1)
                pe.wait_ge(ptc, u + 1)
                if u >= 1:
                    pe.wait_ge(o_read, u)
                for j in range(4):
                    for h in halves:
                        last = mm(aux[1][:, j * HD:(j + 1) * HD], probT[:, u % 2, 4 * h + j, :],
                                  v[:, n - 1 + h, g * HD:(g + 1) * HD], start=(h == halves[0]), stop=(h == 1))
                last.then_inc(o_ready, 1)
                pe.wait_ge(o_read, u + 1)
                if u >= 1:
                    pe.wait_ge(aot_read, u)
                for a in range(2):
                    last = nc.tensor.transpose(aux[1][:, 512 + a * P:512 + (a + 1) * P],
                                               otok[:, u % 2, a * P:(a + 1) * P], ident[:])
                last.then_inc(aot_ready, 1)

            pe.wait_ge(par_in, 16 * 17)
            pe.wait_ge(aot_read, 16)
            for n in range(2):
                for t in range(4):
                    nc.tensor.transpose(aux[n][:, t * P:(t + 1) * P], Cn[:, n, t].rearrange("p a s -> p (a s)"), ident[:]
                                        ).then_inc(ct_ready, 1)
            pe.wait_ge(m1_ready, 1)
            for b in range(4):
                src = (M1r, M1i)[b // 2]
                for a in range(8):
                    last = nc.tensor.transpose((acc + aux)[b][:, a * P:(a + 1) * P],
                                               src[:, (b % 2) * 8 + a].rearrange("p t c -> p (t c)"), ident[:])
                last.then_inc(et_ready, 1)
            pe.wait_ge(et_copied, 2)
            for a in range(PAIRS):
                dst = acc[a // 8][0:32, (a % 8) * P:(a % 8 + 1) * P]
                mm(dst, BBr[:, a].rearrange("p b c -> p (b c)"), FXr[:, a, 0:TAU].rearrange("p t c -> p (t c)"),
                   start=True, stop=False)
                last = mm(dst, BBi[:, a].rearrange("p b c -> p (b c)"), FXi[:, a, 0:TAU].rearrange("p t c -> p (t c)"),
                          start=False, stop=True)
            last.then_inc(k_ready, 1)
            pe.wait_ge(u_in, 16 * TAU)
            pe.wait_ge(k_copied, 1)
            pe.wait_ge(et_copied, 4)
            for h in range(2):
                for a in range(8):
                    for g2 in range(2):
                        pp = slice(g2 * NS, (g2 + 1) * NS)
                        for dst, e in ((acc[h], ETr), (aux[h], ETi)):
                            last = mm(dst[pp, a * P:(a + 1) * P], e[:, 8 * h + a, pp], U[:, 2 * (8 * h + a) + g2, :],
                                      start=True, stop=True)
                last.then_inc(x_ready, 1)
            pe.wait_ge(l_in, 16 * 16)
            pe.wait_ge(h_ready, 1)
            for b in range(4):
                buf = (acc + aux)[b]
                for a in range(4):
                    pr = 4 * b + a
                    for g2 in range(2):
                        pp = slice(g2 * NS, (g2 + 1) * NS)
                        dst = buf[:, g2 * 512 + a * P:g2 * 512 + (a + 1) * P]
                        mm(dst, Lm[:, 2 * pr + g2, :], U[:, 2 * pr + g2, :], start=True, stop=False)
                        mm(dst, FXr[pp, pr, 1:].rearrange("p t c -> p (t c)"), Hr[pp, pr, :], start=False, stop=False)
                        last = mm(dst, FXi[pp, pr, 1:].rearrange("p t c -> p (t c)"), Hi[pp, pr, :], start=False, stop=True)
                last.then_inc(yk_ready, 1)
            pe.wait_ge(y_sb, 4)
            w_tile(START["glu"], ZH, ZL, each=lambda k: pe.wait_ge(zl_ready, k + 1))
            for t in range(1, 4):
                w_tile(START["glu"] + t, ZH, ZL)

            def merge1(i):
                for t in range(4):
                    if t == 2 and first_turn(i):
                        pe.wait_ge(z2l, 4)
                    w_tile(START["merge1"] + t, (AOH, Z2H)[t // 2], (AOL, Z2L)[t // 2], 4, i)
            repeat(pe, 4, merge1)
            w_tile(START["wout"], MH, ML, each=lambda k: pe.wait_ge(ml_ready, k + 1))
            for t in range(1, 8):
                w_tile(START["wout"] + t, MH, ML)
            norm(1)
            norm(2)

            def ff(c):
                for t in range(4):
                    w_tile(START["ff"] + t, YH, YL, 12, c)
                for t in range(4, 12):
                    w_tile(START["ff"] + t, HH, HL, 12, c,
                           each=(lambda k: pe.wait_ge(hl, plus(k + 1, 4, c))) if t == 4 else None)
            repeat(pe, FCH, ff)
            norm(3)
            norm(4)
            for t in range(4):
                token_tile(START["v2"] + t, YH, YL)
            pe.wait_ge(p2_in, 16 * 6)
            for g in range(8):
                last = nc.tensor.transpose(aux[0][:, g * P:(g + 1) * P], wsr[:, g, :], ident[:])
            last.then_inc(ws_t, 1)
            for t in range(8):
                w_tile(START["au"] + t, YH, YL)
            pe.wait_ge(ln_done, MT)
            pe.wait_ge(ws_m, 1)
            for t in range(KW):
                if t >= 2:
                    pe.wait_ge(sg_add, t - 1)
                for n in range(MT):
                    for h in range(2):
                        g = 2 * t + h
                        last = mm(aux[t % 2][h * 64:(h + 1) * 64, n * P:(n + 1) * P], V2[:, n, g * 64:(g + 1) * 64],
                                  wst[:, g, :], start=True, stop=True)
                last.then_inc(sg_ready, 1)

            def merge2(stage, n):
                def turn(i):
                    for t in range(4):
                        w_tile(START[stage] + t, (YH, BH)[t // 2], (YL, BL)[t // 2], 4, i,
                               each=(lambda k: pe.wait_ge(bl, n + k + 1)) if t == 2 and first_turn(i) else None)
                repeat(pe, 4, turn)
            merge2("amerge", 0)
            for t in range(16):
                w_tile(START["bx"] + t, YH, YL)
            merge2("bmerge", 4)
            for t in range(8):
                w_tile(START["cx"] + t, YH, YL)
            for t in range(4):
                pe.wait_ge(bl, 12)
                w_tile(START["pool"] + t, BH[:, t:t + 1, :], BL[:, t:t + 1, :])
            merge2("cmerge", 12)
            pe.wait_ge(nl, 8)
            pe.wait_ge(wo_lo, 4)
            ev_wait(pe, NT - 2)
            ev_wait(pe, NT - 1)
            for m in range(MT):
                pe.wait_ge(x3_in[m % 3], 16 * (m // 3 + 1))
                if m >= 2:
                    pe.wait_ge(o_done, m - 1)
                tk = slice(m * P, (m + 1) * P)
                for h in range(2):
                    sl = slice(512 * h, 512 * (h + 1))
                    for k in range(KD):
                        for w, x in ((WOH, NH), (WOL, NH), (WOH, NL)):
                            last = mm(acc[m % 2][:, sl], x[:, k, tk], w[:, k, sl], start=(k == 0 and w is WOH and x is NH),
                                      stop=(k == KD - 1 and x is NL))
                        if k == 0:
                            for f in range(4 * h, 4 * h + 4):
                                mm(acc[m % 2][:, f * P:(f + 1) * P], xr3[:, m % 3, f, :], ident[:], start=False, stop=False)
                last.then_inc(ot_ready, 1)

        @block.gpsimd
        def _(pool):
            TT = nc.gpsimd.tensor_tensor
            nc.gpsimd.memset(rel[BUCKETS:BUCKETS + 1, :], NEG).then_inc(ones_set, 1)

            def add_square(n, f):
                pool.wait_ge(sq_ready, 8 * n + f + 1)
                if f == 0:
                    if n:
                        pool.wait_ge(rb_ready, n)
                    nc.gpsimd.tensor_copy(ACC[:], S[:, 0, :]).then_inc(sq_added, 1)
                else:
                    pool.wait_ge(sq_added, 8 * n + f)
                    TT(ACC[:], ACC[:], S[:, f % 2, :], ALU.add).then_inc(sq_added, 1)

            def rsqrt(n):
                pool.wait_ge(ms_ready, n + 1)
                pool.wait_ge(const_set, 2)
                TT(rtok, ms, half_neg, ALU.pow).then_inc(rtok_ready, 1)

            for f in range(KD):
                add_square(0, f)
            rsqrt(0)
            pool.wait_ge(s_ready, 16)
            nc.gpsimd.memset(Lm[:], 0.0).then_inc(l_zero, 1)
            for f in range(KD):
                add_square(1, f)
            rsqrt(1)

            def residual(j, n):
                for f in range(KD + 1):
                    if f < KD:
                        pool.wait_ge(f_scaled, 8 * j + f + 1)
                        pool.wait_ge(xr_in[f % 3], 16 * (3 * j - (j if f % 3 == 2 else 0) + f // 3 + 1))
                        TT(F[:, f, :], F[:, f, :], (xr1, xr2)[j][:, f % 3, :], ALU.add).then_inc(x_added, 1)
                    if f >= 1:
                        add_square(n, f - 1)
            residual(0, 2)
            rsqrt(2)
            pool.wait_ge(x_out, 16 * 16)
            pool.wait_ge(xl_ready, 16)
            nc.gpsimd.memset(F[:], 0.0).then_inc(f_zero, 1)
            for f in range(KD):
                add_square(3, f)
            rsqrt(3)
            residual(1, 4)
            rsqrt(4)
            pool.wait_ge(ws_c, 1)
            nc.gpsimd.affine_select(wst[:], wst[:], [[0, 8], [1, P]], ALU.is_ge, 0.0, base=0, channel_multiplier=-1
                                    ).then_inc(ws_m, 1)
            for t in range(MT):
                pool.wait_ge(ln_var, t + 1)
                TT(lnr, lnv, half_neg[:, 0:1], ALU.pow).then_inc(ln_r, 1)
                if t >= 4:
                    pass

            def merge2(stage, n):
                def turn(i):
                    for t in (2, 3):
                        ev_wait(pool, START[stage] + t, 4, i)
                        f = plus(t - 2, 2, i)
                        if n:
                            pool.wait_ge(mg_m, plus(8 * (n - 1) + t - 1, 2, i))
                            TT(row(M, f), row(M, f), S[:, t % 2, :], ALU.add).then_inc(mg_m, 1)
                        else:
                            nc.gpsimd.tensor_copy(row(M, f), S[:, t % 2, :]).then_inc(mg_m, 1)
                repeat(pool, 4, turn)
            merge2("amerge", 0)
            merge2("bmerge", 1)
            merge2("cmerge", 2)
            for m in range(MT):
                pool.wait_ge(fv_r, m + 1)
                TT(fr[:, m:m + 1], fv[:, m:m + 1], half_neg[:, 0:1], ALU.pow).then_inc(fr_r, 1)


INPUTS = ["x", "norm_mix_pre", "norm_mix_post", "norm_mlp_pre", "norm_mlp_post", "w_in", "rel_bias", "sinks", "lam_re",
          "lam_im", "log_dt", "b_re", "b_im", "c_re", "c_im", "d_skip", "w_glu", "w_attn_branch", "w_ssm_branch",
          "w_out", "w_ff_in", "w_ff_out", "norm_g_2", "w_in_2", "ln_g_2", "ln_b_2", "w_s_2", "b_s_2", "conv_w_2",
          "conv_b_2", "w_pool_2", "pool_scale_2", "w_pa_2", "w_pb_2", "w_pc_2", "w_o_2", "final_g_2"]


def shape_constants():
    window = np.array([[w / min(t + 1, w) for t in range(16)] for w in POOLS], np.float32)
    return {"eye": np.eye(P, dtype=np.float32), "eye16": np.tile(np.eye(C, dtype=np.float32), (2, 1)),
            "bucket_rows": bucket_rows(), "window_scale": window}


def kernel(**inputs):
    import concourse.bacc as bacc
    from concourse.bass_utils import run_bass_kernel_spmd

    nc = bacc.Bacc("TRN2", target_bir_lowering=False, num_devices=1)
    arrays = {name: np.ascontiguousarray(inputs[name]) for name in INPUTS}
    arrays.update(shape_constants())
    io = {name: nc.dram_tensor(f"in_{name}", a.shape, mybir.dt.from_np(a.dtype), kind="ExternalInput").ap()
          for name, a in arrays.items()}
    out = nc.dram_tensor("out", (1, SEQ, D), mybir.dt.float32, kind="ExternalOutput").ap()
    hybrid_kernel(nc, io, out)
    r = run_bass_kernel_spmd(nc, [{f"in_{name}": a for name, a in arrays.items()}], core_ids=[0])
    return r.results[0]["out"]
```

```python
import concourse.bass as bass
from concourse import mybir
from contextlib import ExitStack
import numpy as np

P = 128
SEQ, D = 1024, 1024
KD = D // P
MT = SEQ // P
HEADS, KV, HD = 8, 2, 64
BUCKETS, WINDOW, MAXD = 32, 128, 128
G, C, NS = 32, 16, 64
TAU = 8
CH = SEQ // TAU
PAIRS = G // 2
W4 = 512
KW = W4 // P
FF = 4096
FCH = FF // W4
CONV = 3
POOLS = (2, 4, 8, 16)
RMS_EPS, LN_EPS = 1e-6, 1e-5
NEG = -1e30
ROWLEN = 3 * P

STAGES = [("q", 4, 8), ("kv", 2, 8), ("gate1", 16, 8), ("u", 4, 8), ("glu", 4, 4), ("merge1", 16, 4),
          ("wout", 8, 8), ("ff", 12 * FCH, 0), ("v2", 4, 8), ("au", 4, 8), ("az", 4, 8), ("amerge", 16, 0),
          ("bx", 4, 8), ("bc", 4, 8), ("bb", 4, 8), ("bz", 4, 8), ("bmerge", 16, 0),
          ("cx", 4, 8), ("cz", 4, 8), ("pool", 4, 1), ("cmerge", 16, 0)]
START, KOF = {}, []
for _name, _n, _k in STAGES:
    START[_name] = len(KOF)
    if _name == "ff":
        KOF += ([8] * 4 + [4] * 8) * FCH
    elif _k == 0:
        KOF += [8, 8, 4, 4] * 4
    else:
        KOF += [_k] * _n
NT = len(KOF)
A_U, A_V, A_Z, B_X, B_B, B_C, B_Z, C_X, C_Z, G_A, G_B, G_C = [0, 512, 1024, 1536, 2048, 2560, 3072, 3584, 4096,
                                                              4608, 5632, 6656]


def bucket_rows():
    rows = np.zeros((BUCKETS + 1, ROWLEN), np.float32)
    half = BUCKETS // 2
    for m in range(ROWLEN):
        d = 2 * P - 1 - m
        if not 0 <= d < WINDOW:
            rows[BUCKETS, m] = 1.0
            continue
        b = d
        if d >= half:
            b = min(half + int(np.log(d / half) / np.log(MAXD / half) * (BUCKETS - half)), BUCKETS - 1)
        rows[b, m] = 1.0
    return rows


def hybrid_kernel(nc, io, out):
    f32, f32r = mybir.dt.float32, mybir.dt.float32r
    ALU, ACT, AX = mybir.AluOpType, mybir.ActivationFunctionType, mybir.AxisListType
    ds = bass.ds
    KB = 1024
    ctx = ExitStack()
    with ctx:
        arena = ctx.enter_context(nc.sbuf_tensor("arena", [P, 207 * 256], f32))
        ORIGIN = nc.sbuf_base - 207 * KB

        def at(name, shape, kib, dt=f32):
            return nc.alloc_sbuf_tensor_at(name, shape, dt, offset=ORIGIN + int(kib * KB))

        def sem(name):
            return ctx.enter_context(nc.semaphore(name))

        def dram(name, shape):
            return nc.dram_tensor(name, shape, f32, kind="Internal").ap()

        raw = at("raw", [P, 2, KD, 2 * P], 0)
        WH = at("WH", [P, 2, KD, P], 16, f32r)
        WL = at("WL", [P, 2, KD, P], 24, f32r)
        vec = at("vec", [P, 448], 32)
        RA = at("RA", [P, SEQ], 34)
        RP = at("RP", [P, SEQ], 38)
        ACC = at("ACC", [P, SEQ], 42)
        S = at("S", [P, 2, SEQ], 46)
        ident = at("ident", [P, P], 54)
        ones = at("ones", [P, P], 54.5)
        small = at("small", [P, 256], 55)
        XH, XL = at("XH", [P, KD, SEQ], 56, f32r), at("XL", [P, KD, SEQ], 88, f32r)
        XT = at("XT", [P, KD, SEQ], 120)
        xtok = at("xtok", [P, MT, D], 152)
        q, k_, v = at("q", [P, 4, SEQ], 120), at("k", [P, SEQ], 136), at("v", [P, MT, P], 140)
        gst = at("gst", [P, 2, SEQ], 184)
        ust = at("ust", [P, 2, SEQ], 192)
        AOH, AOL = at("AOH", [P, KW, SEQ], 56, f32r), at("AOL", [P, KW, SEQ], 72, f32r)
        bias = at("bias", [P, HEADS, 2 * P], 184)
        prob = at("prob", [P, 2, 4, 2 * P], 96)
        QH, QL = at("QH", [P, 4, SEQ], 104, f32r), at("QL", [P, 4, SEQ], 120, f32r)
        KH, KL = at("KH", [P, SEQ], 46, f32r), at("KL", [P, SEQ], 136, f32r)
        VH, VL = at("VH", [P, MT, P], 50, f32r), at("VL", [P, MT, P], 140, f32r)
        PTH, PTL = at("PTH", [P, 2, 2, 4, P], 16, f32r), at("PTL", [P, 2, 2, 4, P], 24, f32r)
        bsel = at("bsel", [BUCKETS + 1, ROWLEN], 184)
        rel = at("rel", [BUCKETS + 1, HEADS], 186)
        brow = at("brow", [HEADS, ROWLEN], 187)
        U = at("U", [P, G, CH], 104)
        ETr, ETi = at("ETr", [P, PAIRS, P], 88), at("ETi", [P, PAIRS, P], 96)
        Lm = at("Lm", [P, G, P], 120)
        FXr, FXi = at("FXr", [P, PAIRS, TAU + 1, C], 144), at("FXi", [P, PAIRS, TAU + 1, C], 153)
        RC, RS = at("RC", [P, PAIRS, CH], 162), at("RS", [P, PAIRS, CH], 170)
        Dk = at("Dk", [P, PAIRS, CH], 136)
        Kt = at("Kt", [32, PAIRS, P], 38)
        Vr, Vi = at("Vr", [P, PAIRS, CH], 184), at("Vi", [P, PAIRS, CH], 192)
        M1r, M1i = at("M1r", [P, PAIRS, TAU, C], 88), at("M1i", [P, PAIRS, TAU, C], 192)
        Cn = at("Cn", [P, 2, 4, 2, NS], 178)
        BBr, BBi = at("BBr", [P, PAIRS, 2, C], 178), at("BBi", [P, PAIRS, 2, C], 180)
        Cr, nCi = at("Cr", [P, PAIRS, C], 182), at("nCi", [P, PAIRS, C], 183)
        Br, Bi = at("Br", [P, PAIRS, C], 200), at("Bi", [P, PAIRS, C], 201)
        Bbr, Bbi = at("Bbr", [P, PAIRS, C], 202), at("Bbi", [P, PAIRS, C], 203)
        kd = at("kd", [32, PAIRS, C], 200)
        lam = at("lam", [P, 24, PAIRS], 204)
        Ar, Ai = at("Ar", [P, TAU + 1, PAIRS], 205.5), at("Ai", [P, TAU + 1, PAIRS], 206.0625)
        dsk = at("dsk", [32, PAIRS], 206.625)
        eye16 = at("eye16", [32, C], 206.75)
        ct = at("ct", [P, 4, 256], 42)
        rt = at("rt", [P, 2, PAIRS * CH // 4], 38)
        Hr, Hi = at("Hr", [P, PAIRS, CH], 88), at("Hi", [P, PAIRS, CH], 96)
        Ysb = at("Ysb", [P, G, CH], 184)
        Z = at("Z", [P, KW, SEQ], 168)
        ZH, ZL = at("ZH", [P, KW, SEQ], 104, f32r), at("ZL", [P, KW, SEQ], 120, f32r)
        Z2H, Z2L = at("Z2H", [P, KW, SEQ], 136, f32r), at("Z2L", [P, KW, SEQ], 152, f32r)
        gin = at("gin", [P, 4, SEQ], 120)
        MH, ML = at("MH", [P, KD, SEQ], 88, f32r), at("ML", [P, KD, SEQ], 168, f32r)
        F = at("F", [P, KD, SEQ], 56)
        YH, YL = at("YH", [P, KD, SEQ], 88, f32r), at("YL", [P, KD, SEQ], 120, f32r)
        xr1 = at("xr1", [P, 3, SEQ], 152)
        HH, HL = at("HH", [P, KW, SEQ], 152, f32r), at("HL", [P, KW, SEQ], 168, f32r)
        xr2 = at("xr2", [P, 3, SEQ], 184)
        V2 = at("V2", [P, MT, W4], 56)
        wst = at("wst", [P, 8, P], 72)
        lng, lnb = at("lng", [P, W4], 80), at("lnb", [P, W4], 82)
        bsb = at("bsb", [P, KW, P], 84)
        wsr = at("wsr", [P, 8, P], 152)
        M = at("M", [P, KD, SEQ], 56)
        BH, BL = at("BH", [P, KW, SEQ], 152, f32r), at("BL", [P, KW, SEQ], 168, f32r)
        Y = at("Y", [P, KW, SEQ], 184)
        Gb = [ACC, at("G1", [P, SEQ], 200)]
        cnt = at("cnt", [P, KW, 16], 204)
        WOH, WOL = at("WOH", [P, KD, D], 88, f32r), at("WOL", [P, KD, D], 120, f32r)
        NHs = [at("NH0", [P, KW, SEQ], 184, f32r), at("NH1", [P, KW, SEQ], 152, f32r)]
        NL = at("NL", [P, KD, SEQ], 56, f32r)
        xr3 = at("xr3", [P, 3, KD, P], 168)
        fgb = at("fgb", [P, D], 180)

        def column(n, at_=[0]):
            at_[0] += n
            return vec[:, at_[0] - n:at_[0]]

        g_pre1, g_post1, g_pre2, g_post2, g_pre3 = [column(KD) for _ in range(5)]
        cw, cb, psc = column(CONV * KW), column(KW), column(KW)
        sink = column(HEADS)
        one_col, half_neg = column(1), column(KD)
        ms, rtok = column(KD), column(KD)
        mx, nm, den, es, rd = [column(8) for _ in range(5)]
        bn, ag, lnr = column(6), column(2), column(1)
        lnv = column(1)
        ss, fv, fr = column(MT), column(MT), column(MT)

        acc = [ctx.enter_context(nc.psum_tensor(f"acc{i}", [P, 1024], f32)) for i in range(2)]
        aux = [ctx.enter_context(nc.psum_tensor(f"aux{i}", [P, 1024], f32)) for i in range(2)]

        halves_x = ((acc[0], aux[0]), (acc[1], aux[1]))
        ybuf = [acc[0], aux[0], acc[1], aux[1]]

        x_scr = [dram(f"x_scr{i}", [D, SEQ]) for i in range(3)]
        g_scr = dram("g_scr", [16 * P, SEQ])
        u_scr, y_scr = dram("u_scr", [W4, SEQ]), dram("y_scr", [W4, SEQ])
        b_scr = dram("b_scr", [HEADS, P, ROWLEN])

        w_in_s = [sem("w_loaded0"), sem("w_loaded1")]
        w_hi, w_lo, tile_done = sem("w_hi"), sem("w_lo"), sem("tile_done")
        evicted = [sem("evicted0"), sem("evicted1")]
        constants_loaded, id_in, bs_in = sem("constants_loaded"), sem("identity_loaded"), sem("bucket_rows_loaded")
        x_in = [sem(f"x{m}_loaded") for m in range(MT)]
        xt_ready, xt_evicted_act, xt_evicted_dve = sem("xt_ready"), sem("xt_evicted_act"), sem("xt_evicted_dve")
        ones_set, const_set = sem("ones_set"), sem("const_set")
        xh_ready, xl_ready = sem("xh_ready"), sem("xl_ready")
        sq_ready, sq_added = sem("sq_ready"), sem("sq_added")
        mean_ready, ms_ready, rtok_ready = sem("mean_ready"), sem("ms_ready"), sem("rtok_ready")
        rdg_ready, rb_ready = sem("rdiag_ready"), sem("rb_ready")
        x_out = sem("residual_stored")
        dchain, pchain, achain = sem("dve_chain"), sem("pool_chain"), sem("act_chain")
        gate_ready = sem("gate_ready")
        g_out = [sem("gate_stored0"), sem("gate_stored1")]
        u_out, u_in = [sem("u_stored0"), sem("u_stored1")], sem("u_loaded")
        b_row, b_rowsb, b_out, b_in = sem("b_row"), sem("b_row_copied"), sem("b_stored"), sem("b_loaded")
        s_ready, s_read, nm_ready, p_ready = sem("s_ready"), sem("s_read"), sem("nm_ready"), sem("p_ready")
        pn_ready, pt_ready, pt_hi, pt_lo = sem("p_normalised"), sem("pt_ready"), sem("pt_hi"), sem("pt_lo")
        o_ready, ao_hi, ao_lo = sem("o_ready"), sem("ao_hi"), sem("ao_lo")
        kv_hi, kv_lo, q_hi, q_lo = sem("kv_hi"), sem("kv_lo"), sem("q_hi"), sem("q_lo")
        ssm_loaded = sem("ssm_loaded")
        dt_ready, angle_ready, trig_ready = sem("dt_ready"), sem("angle_ready"), sem("trig_ready")
        ct_ready, c_ready, rot_ready = sem("c_transposed"), sem("c_copied"), sem("rotations_ready")
        m1_ready, et_ready, et_copied = sem("m1_ready"), sem("et_ready"), sem("et_copied")
        k_ready, kt_copied, k_copied, l_zero = sem("k_ready"), sem("kernels_copied"), sem("skip_added"), sem("l_zero")
        l_in = sem("l_filled")
        x_ready, h_ready, yk_ready = sem("x_ready"), sem("h_ready"), sem("yk_ready")
        y_sb = sem("y_copied")
        y_out, z_in = [sem("y_stored0"), sem("y_stored1")], [sem(f"z{b}_loaded") for b in range(KW)]
        z_act, zh_ready, zl_ready = sem("z_act"), sem("zh_ready"), sem("zl_ready")
        glu_mul, z2h, z2l = sem("glu_mul"), sem("z2_hi"), sem("z2_lo")
        ga_in = [sem(f"gin{i}") for i in range(4)]
        m_sum, mh_ready, ml_ready = sem("m_sum"), sem("mh_ready"), sem("ml_ready")
        f_scaled, x_added = sem("f_scaled"), sem("x_added")
        xr_in = [sem(f"xr{i}_loaded") for i in range(3)]
        f_zero, f_final = sem("f_zero"), sem("f_final")
        hidden_squared, hidden_hi, hidden_lo = sem("hidden_squared"), sem("hidden_hi"), sem("hidden_lo")
        vt_ready, v_copied, v2_gelu, vt2_ready = sem("vt_ready"), sem("v_copied"), sem("v2_gelu"), sem("vt2_ready")
        v2_copied, ln_var, ln_r, ln_done = sem("v2_copied"), sem("ln_var"), sem("ln_r"), sem("ln_done")
        block2_loaded, ws_t, ws_c, ws_m = sem("p2_loaded"), sem("ws_t"), sem("ws_copied"), sem("ws_masked")
        a_gelu, a_product = sem("a_gelu"), sem("a_product")
        sg_ready, sg_add, sg_mul = sem("sg_ready"), sem("sg_added"), sem("sg_mul")
        branch_hi, branch_lo = sem("branch_hi"), sem("branch_lo")
        gate_made, m_added = sem("mg_gate"), sem("mg_added")
        b_convolved, b_gated, b_silu, b_product = sem("b_convolved"), sem("b_gated"), sem("b_silu"), sem("b_product")
        c_pooled, c_silu = sem("c_pooled"), sem("c_silu")
        m_hi, m_lo, wo_hi, wo_lo = sem("nh_ready"), sem("nl_ready"), sem("wo_hi"), sem("wo_lo")
        fg_loaded, fsum, fv_r, fr_r = sem("fg_loaded"), sem("out_sum"), sem("fv"), sem("fr")
        o_done = sem("out_ready")
        ot_ready = sem("ot_ready")
        stored = [sem("stored0"), sem("stored1")]
        x3_in = [sem(f"x3_{i}") for i in range(3)]

        block = ctx.enter_context(nc.Block())

        def row(t, f):
            return t[:, f, :] if isinstance(f, int) else t[:, ds(f, 1), :].rearrange("p o n -> p (o n)")

        def perm(t):
            return t.rearrange("p (h t) -> p t h", t=TAU)

        def unperm(t):
            return t.rearrange("p (t h) -> p t h", t=TAU)

        def repeat(eng, n, body):
            body(0)
            with eng.Fori(1, n - 1) as i:
                body(i)
            body(n - 1)

        def plus(base, per, i):
            return base + per * i

        def first_turn(i):
            return isinstance(i, int) and i == 0

        def ev(T0):
            return evicted[T0 % 2]

        def ev_wait(eng, T0, per=0, i=0):
            eng.wait_ge(evicted[T0 % 2], plus(T0 // 2 + 1, per // 2, i))

        @block.sync
        def _(sp):
            def panel(p0, src, kb, per=0, i=0):
                if p0 >= 2:
                    sp.wait_ge(w_lo, plus(2 * (p0 - 1), 2 * per, i))
                sp.dma_start(raw[:, p0 % 2, 0:kb, :], src).then_inc(w_in_s[p0 % 2], 16)

            def cols(w, c, n=2 * P):
                return w[:, :, ds(c, n)] if not isinstance(c, int) else w[:, :, c:c + n]

            w1 = io["w_in"].rearrange("o (k p) n -> p (o k) n", p=P)
            w2 = io["w_in_2"].rearrange("o (k p) n -> p (o k) n", p=P)
            xt_ = io["x"].rearrange("b (m p) d -> p (b m) d", p=P)
            for m in range(MT):
                sp.dma_start(xtok[:, m, :], xt_[:, m, :]).then_inc(x_in[m], 16)
                if m == MT - 1:
                    qw = io["w_in"][:, :, 0:512].rearrange("o (k p) (a j d) -> a j p (o k) d", p=P, a=2, d=HD)
                    for pp in range(2):
                        for j in range(2):
                            for a in range(2):
                                sp.dma_start(raw[:, pp, :, j * P + a * HD:j * P + (a + 1) * HD],
                                             qw[a, 2 * pp + j]).then_inc(w_in_s[pp], 16)
            panel(START["kv"] // 2, cols(w1, 512), 8)
            sp.wait_ge(xt_ready, MT)
            with nc.allow_non_contiguous_dma("small parameters"):
                for g2 in range(2):
                    dst = slice(g2 * NS, (g2 + 1) * NS)
                    for n, name in enumerate(("lam_re", "lam_im")):
                        sp.dma_start(lam[dst, n, :], io[name].rearrange("o (a b) s -> (o b) s a", b=2)[g2]
                                     ).then_inc(ssm_loaded, 16)
                    sp.dma_start(lam[dst, 2, :], bass.AP(io["log_dt"].tensor, g2, [[0, NS], [2, PAIRS]])
                                 ).then_inc(ssm_loaded, 16)
                    sp.dma_start(dsk[g2 * C:(g2 + 1) * C, :],
                                 io["d_skip"].rearrange("o (a b c) -> (o b) c a", b=2, c=C)[g2]).then_inc(ssm_loaded, 16)
                    sp.dma_start(Br[dst], io["b_re"].rearrange("o (a b) s c -> (o b) s a c", b=2)[g2]
                                 ).then_inc(ssm_loaded, 16)
                    sp.dma_start(Bi[dst], io["b_im"].rearrange("o (a b) s c -> (o b) s a c", b=2)[g2]
                                 ).then_inc(ssm_loaded, 16)
                for n, name in enumerate(("c_re", "c_im")):
                    for dup in range(2):
                        sp.dma_start(Cn[:, n, :, dup, :], io[name].rearrange("o (t g) c s -> (g c) (o t) s", g=8)
                                     ).then_inc(ssm_loaded, 16)
            sp.dma_start(eye16[:], io["eye16"]).then_inc(ssm_loaded, 16)
            G0 = 512 + 2 * P + W4

            def gate_panels(i):
                for h in range(2):
                    panel(START["gate1"] // 2 + h, cols(w1, plus(G0 + h * 256, 512, i)), 8, 2, i)
            for i in range(4):
                gate_panels(i)
            for h in range(2):
                panel(START["u"] // 2 + h, cols(w1, 768 + 256 * h), 8)
            sp.wait_ge(b_out, 16)
            for n in range(2):
                sp.wait_ge(g_out[n], 16 * 8)
            sp.dma_start(bias[:], bass.AP(b_scr.tensor, P - 1, [[ROWLEN - 1, P], [P * ROWLEN, HEADS], [1, 2 * P]])
                         ).then_inc(b_in, 16)
            wg = io["w_glu"].rearrange("o (k p) n -> p (o k) n", p=P)
            for h in range(2):
                panel(START["glu"] // 2 + h, cols(wg, 256 * h), 4)
            for n in range(2):
                sp.wait_ge(u_out[n], 32)
            sp.wait_ge(s_ready, 16)
            uv = u_scr.rearrange("(g c) (t h) -> t c g h", c=C, t=TAU)
            for t in range(TAU):
                sp.dma_start(U[t * C:(t + 1) * C], uv[t]).then_inc(u_in, 16)
            sp.wait_ge(l_zero, 1)
            sp.wait_ge(k_copied, 1)
            Lv = Lm[:].rearrange("p (a b) m -> p a b m", b=2)
            for t in range(TAU):
                for g2 in range(2):
                    sp.dma_start(Lv[t * C:(t + 1) * C, :, g2, t * C:P], Kt[g2 * C:(g2 + 1) * C, :, 0:P - t * C]
                                 ).then_inc(l_in, 16)
            yv = y_scr.rearrange("(g c) (t h) -> t c g h", c=C, t=TAU)
            for b in range(KW):
                sp.wait_ge(y_sb, b + 1)
                for t in range(TAU):
                    sp.dma_start(yv[t][:, 8 * b:8 * b + 8], Ysb[t * C:(t + 1) * C, 8 * b:8 * b + 8]
                                 ).then_inc(y_out[b % 2], 16)
                if b == 0:
                    sp.wait_ge(h_ready, 2)
                sp.wait_ge(y_out[b % 2], 16 * TAU * (b // 2 + 1))
                sp.dma_start(Z[:, b, :], y_scr[b * P:(b + 1) * P, :]).then_inc(z_in[b], 16)
            wa = io["w_attn_branch"].rearrange("o (g j d) n -> g d (o j) n", g=KV, d=HD)
            wsb = io["w_ssm_branch"].rearrange("o (k p) n -> p (o k) n", p=P)
            gv = g_scr.rearrange("(f p) t -> p f t", p=P)
            sp.wait_ge(g_out[0], 16 * 8)
            sp.wait_ge(g_out[1], 16 * 8)
            sp.wait_ge(tile_done, START["merge1"])

            def merge_loads(i):
                p0 = START["merge1"] // 2
                sp.wait_ge(w_lo, plus(2 * (p0 - 1), 4, i))
                for g in range(KV):
                    sp.dma_start(raw[g * HD:(g + 1) * HD, p0 % 2, 0:4, :], wa[g][:, :, 256 * i:256 * (i + 1)]
                                 ).then_inc(w_in_s[p0 % 2], 16)
                for h in range(2):
                    for n in range(2):
                        ev_wait(sp, START["merge1"] - 4 + 2 * n + h, 4, i)
                        f = plus(n * 8 + h, 2, i)
                        sp.dma_start(gin[:, 2 * n + h, :], row(gv, f)).then_inc(ga_in[2 * n + h], 16)
                panel(START["merge1"] // 2 + 1, cols(wsb, plus(0, 256, i)), 4, 2, i)
            for i in range(4):
                merge_loads(i)
            wo1 = io["w_out"].rearrange("o (k p) n -> p (o k) n", p=P)
            for h in range(4):
                panel(START["wout"] // 2 + h, cols(wo1, 256 * h), 8)
            sp.wait_ge(tile_done, START["wout"])

            def residual(j, src, ring):
                sp.wait_ge(x_out, 16 * 8 * (j + 1))
                for f in range(KD):
                    n = 8 * j + f
                    if f >= 3:
                        sp.wait_ge(x_added, n - 2)
                    sp.dma_start(ring[:, f % 3, :], row(src.rearrange("(f p) t -> p f t", p=P), f)
                                 ).then_inc(xr_in[f % 3], 16)
            wf1 = io["w_ff_in"].rearrange("o (k p) n -> p (o k) n", p=P)
            wf2 = io["w_ff_out"].rearrange("o (c k p) n -> p (o c k) n", p=P, k=KW)
            panel(START["ff"] // 2, cols(wf1, 0), 8)
            residual(0, x_scr[0], xr1)

            def ff_panels(c):
                for h in range(1 if c == 0 else 0, 2):
                    panel(START["ff"] // 2 + h, cols(wf1, plus(256 * h, 512, c)), 8, 6, c)
                for h in range(4):
                    src = wf2[:, ds(c * KW, KW), 256 * h:256 * (h + 1)] if not isinstance(c, int) else \
                        wf2[:, c * KW:(c + 1) * KW, 256 * h:256 * (h + 1)]
                    panel(START["ff"] // 2 + 2 + h, src, 4, 6, c)
            for c in range(FCH):
                ff_panels(c)
            panel(START["v2"] // 2, cols(w2, A_V), 8)
            sp.wait_ge(f_final, 1)
            residual(1, x_scr[1], xr2)
            sp.wait_ge(tile_done, START["v2"])
            sp.dma_start(wsr[:], io["w_s_2"].rearrange("o g t s -> t (o g) s")).then_inc(block2_loaded, 16)
            panel(START["v2"] // 2 + 1, cols(w2, A_V + 256), 8)
            sp.wait_ge(xl_ready, 24)
            sp.wait_ge(sq_ready, 40)
            sp.wait_ge(x_out, 16 * 24)
            sp.dma_start(lng[:], bass.AP(io["ln_g_2"].tensor, 0, [[0, P], [1, W4]])).then_inc(block2_loaded, 16)
            sp.dma_start(cnt[:], bass.AP(io["window_scale"].tensor, 0, [[0, P], [1, KW * 16]]).rearrange(
                "p (t w) -> p t w", t=KW)).then_inc(block2_loaded, 16)
            sp.dma_start(lnb[:], bass.AP(io["ln_b_2"].tensor, 0, [[0, P], [1, W4]])).then_inc(block2_loaded, 16)
            for h in range(2):
                sp.dma_start(bsb[h * 64:(h + 1) * 64],
                             bass.AP(io["b_s_2"].tensor, h * P, [[0, 64], [2 * P, KW], [1, P]])).then_inc(block2_loaded, 16)
            for name, col in (("au", A_U), ("az", A_Z)):
                for h in range(2):
                    panel(START[name] // 2 + h, cols(w2, col + 256 * h), 8)

            def branch_panels(stage, gate_col, wname):
                wp = io[wname].rearrange("o (k p) n -> p (o k) n", p=P)

                def turn(i):
                    panel(START[stage] // 2, cols(w2, plus(gate_col, 256, i)), 8, 2, i)
                    panel(START[stage] // 2 + 1, cols(wp, plus(0, 256, i)), 4, 2, i)
                for i in range(4):
                    turn(i)
            branch_panels("amerge", G_A, "w_pa_2")
            for name, col in (("bx", B_X), ("bc", B_C), ("bb", B_B), ("bz", B_Z)):
                for h in range(2):
                    panel(START[name] // 2 + h, cols(w2, col + 256 * h), 8)
            branch_panels("bmerge", G_B, "w_pb_2")
            for name, col in (("cx", C_X), ("cz", C_Z)):
                for h in range(2):
                    panel(START[name] // 2 + h, cols(w2, col + 256 * h), 8)
            for h in range(2):
                p0 = START["pool"] // 2 + h
                sp.wait_ge(w_lo, 2 * (p0 - 1))
                sp.dma_start(raw[:, p0 % 2, 0, :].rearrange("p (g d) -> p g d", g=2),
                             io["w_pool_2"][0, 2 * h:2 * h + 2].rearrange("g c d -> c g d")).then_inc(w_in_s[p0 % 2], 16)
            branch_panels("cmerge", G_C, "w_pc_2")
            wo2 = io["w_o_2"].rearrange("o (k p) n -> p (o k) n", p=P)
            for i in range(4):
                p0 = NT // 2 + i
                if i < 2:
                    sp.wait_ge(w_lo, 2 * (p0 - 1))
                else:
                    sp.wait_ge(wo_lo, i - 1)
                sp.dma_start(raw[:, p0 % 2], cols(wo2, 256 * i)).then_inc(w_in_s[p0 % 2], 16)
            sp.wait_ge(tile_done, NT)
            sp.wait_ge(m_added, 24)
            sp.dma_start(fgb[:], bass.AP(io["final_g_2"].tensor, 0, [[0, P], [1, D]])).then_inc(fg_loaded, 16)
            x2v = x_scr[2].rearrange("(k p) (m t) -> m p k t", p=P, t=P)
            for m in range(3):
                sp.dma_start(xr3[:, m], x2v[m]).then_inc(x3_in[m], 16)
            for m in range(MT):
                if m + 3 < MT:
                    sp.wait_ge(ot_ready, m + 1)
                    sp.dma_start(xr3[:, m % 3], x2v[m + 3]).then_inc(x3_in[m % 3], 16)
                sp.wait_ge(o_done, m + 1)
                sp.dma_start(out[0, m * P:(m + 1) * P, :], S[:, m % 2, :]).then_inc(stored[m % 2], 16)
            for n in range(2):
                sp.wait_ge(stored[n], 8 * MT)

        @block.scalar
        def _(act):
            def w_count(T0):
                p0, pa = T0 // 2, START["merge1"] // 2
                attn = min((p0 - pa) // 2 + 1, 4) if p0 >= pa and (p0 - pa) % 2 == 0 else 0
                return 16 * (4 + p0 // 2 + attn)

            def hi(T0, per=0, i=0):
                if T0 >= NT:
                    return
                two = START["merge1"] <= T0 < START["merge1"] + 16 and (T0 - START["merge1"]) % 4 < 2
                act.wait_ge(w_in_s[(T0 // 2) % 2], plus(w_count(T0), per // 4 * 16 * (2 if two else 1), i))
                if T0 >= 2:
                    act.wait_ge(tile_done, plus(T0 - 1, per, i))
                kb = KOF[T0]
                nc.scalar.activation(WH[:, T0 % 2, 0:kb, :],
                                     raw[:, (T0 // 2) % 2, 0:kb, (T0 % 2) * P:(T0 % 2 + 1) * P], ACT.Copy
                                     ).then_inc(w_hi, 1)

            def hi_next(T0, per, i):
                hi(T0 + 1 + per * i) if isinstance(i, int) else hi(T0 + 1, per, i)

            act.dma_start(ident[:], io["eye"]).then_inc(id_in, 16)
            act.dma_start(bsel[:], io["bucket_rows"]).then_inc(bs_in, 16)
            act.dma_start(rel[0:BUCKETS], io["rel_bias"]).then_inc(bs_in, 16)
            with nc.allow_non_contiguous_dma("small parameters"):
                for dst, name in ((g_pre1, "norm_mix_pre"), (g_post1, "norm_mix_post"), (g_pre2, "norm_mlp_pre"),
                                  (g_post2, "norm_mlp_post"), (g_pre3, "norm_g_2")):
                    act.dma_start(dst, io[name].rearrange("o (k p) -> p (o k)", p=P)).then_inc(constants_loaded, 16)
                act.dma_start(cw.rearrange("p (j t) -> p j t", j=CONV),
                              io["conv_w_2"].rearrange("o j (t p) -> p (o j) t", p=P)).then_inc(constants_loaded, 16)
                act.dma_start(cb, io["conv_b_2"].rearrange("o (t p) -> p (o t)", p=P)).then_inc(constants_loaded, 16)
                act.dma_start(psc, io["pool_scale_2"].rearrange("o (t p) -> p (o t)", p=P)).then_inc(constants_loaded, 16)
                act.dma_start(sink, bass.AP(io["sinks"].tensor, 0, [[0, P], [1, HEADS]])).then_inc(constants_loaded, 16)

            for m in range(0, MT, 2):
                act.wait_ge(xt_ready, m + 1)
                nc.scalar.activation(XT[:, :, m * P:(m + 1) * P], aux[0][:].rearrange("p (k t) -> p k t", k=KD),
                                     ACT.Copy).then_inc(xt_evicted_act, 1)
            hi(0)
            act.wait_ge(b_row, 1)
            nc.scalar.activation(brow[:], aux[1][0:HEADS, 0:ROWLEN], ACT.Copy).then_inc(b_rowsb, 1)
            act.wait_ge(b_rowsb, 1)
            act.dma_start(b_scr, brow[:].rearrange("h (o m) -> h o m", o=1).to_broadcast([HEADS, P, ROWLEN])
                          ).then_inc(b_out, 16)
            act.wait_ge(constants_loaded, 144)
            act.wait_ge(xt_evicted_act, 4)
            act.wait_ge(xt_evicted_dve, 4)

            def square(src, f, n):
                if 8 * n + f >= 2:
                    act.wait_ge(sq_added, 8 * n + f - 1)
                nc.scalar.activation(S[:, f % 2, :], src[:, f, :], ACT.Square).then_inc(sq_ready, 1)

            def split_input(src, dst, gain, scr, j, n):
                for f in range(KD):
                    if j:
                        act.wait_ge(x_added, 8 * (j - 1) + f + 1)
                    nc.scalar.activation(dst[:, f, :], src[:, f, :], ACT.Copy, scale=gain[:, f:f + 1]
                                         ).then_inc(xh_ready, 1)
                    if j:
                        square(src, f, n)
                        act.dma_start(scr[f * P:(f + 1) * P, :], src[:, f, :]).then_inc(x_out, 16)
            split_input(XT, XH, g_pre1, x_scr[0], 0, 0)
            hi(1)
            for f in range(KD):
                square(XT, f, 0)
                act.dma_start(x_scr[0][f * P:(f + 1) * P, :], XT[:, f, :]).then_inc(x_out, 16)

            for T in range(1, START["gate1"]):
                hi(T + 1)
                if T == 3:
                    act.wait_ge(ssm_loaded, 16 * 17)
                    nc.scalar.activation(lam[:, 3, :], lam[:, 2, :], ACT.Exp).then_inc(dt_ready, 1)
                elif T == 4:
                    act.wait_ge(angle_ready, 1)
                    nc.scalar.activation(lam[:, 5, :], lam[:, 4, :], ACT.Exp).then_inc(trig_ready, 1)
                elif T == 5:
                    act.wait_ge(angle_ready, 3)
                    nc.scalar.activation(lam[:, 12, :], lam[:, 10, :], ACT.Sin).then_inc(trig_ready, 1)
                    nc.scalar.activation(lam[:, 13, :], lam[:, 11, :], ACT.Sin).then_inc(trig_ready, 1)
            act.wait_ge(b_out, 16)

            def gates(i):
                for t in range(4):
                    T0 = START["gate1"] + t
                    hi_next(T0, 4, i)
                    if t == 0 and first_turn(i):
                        act.wait_ge(vt_ready, 1)
                        nc.scalar.activation(v[:], aux[0][:].rearrange("p (m n) -> p m n", m=MT), ACT.Copy
                                             ).then_inc(v_copied, 1)
                    ev_wait(act, T0, 4, i)
                    if t >= 2 or not first_turn(i):
                        act.wait_ge(g_out[t % 2], plus(16 * (t // 2), 32, i))
                    nc.scalar.activation(gst[:, t % 2, :], S[:, t % 2, :], ACT.Sigmoid).then_inc(gate_ready, 1)
                    act.wait_ge(gate_ready, plus(t + 1, 4, i))
                    gd = g_scr.rearrange("(f p) t -> p f t", p=P)
                    act.dma_start(row(gd, plus(t, 4, i)), gst[:, t % 2, :]).then_inc(g_out[t % 2], 16)
            repeat(act, 4, gates)
            def split_q(c):
                sl = slice(256 * c, 256 * (c + 1))
                nc.scalar.activation(QH[:, :, sl], q[:, :, sl], ACT.Copy).then_inc(q_hi, 1)

            for t in range(4):
                if t < 3:
                    hi(START["u"] + t + 1)
                if t == 0:
                    act.wait_ge(v_copied, 1)
                    nc.scalar.activation(KH[:], k_[:], ACT.Copy).then_inc(kv_hi, 1)
                    nc.scalar.activation(VH[:], v[:], ACT.Copy).then_inc(kv_hi, 1)
                if t == 3:
                    act.wait_ge(tile_done, START["glu"])
                    split_q(0)
                ev_wait(act, START["u"] + t)
                act.dma_start(u_scr[t * P:(t + 1) * P, :], ust[:, t % 2, :]).then_inc(u_out[t % 2], 16)
            units = [(n, g) for n in range(MT) for g in range(KV)]

            def exps(u):
                n, g = units[u]
                lo = P if n == 0 else 0
                act.wait_ge(nm_ready, u + 1)
                c = 4 * (u % 2)
                for j in range(4):
                    nc.scalar.activation(prob[:, u % 2, j, lo:], prob[:, u % 2, j, lo:], ACT.Exp,
                                         bias=nm[:, c + j:c + j + 1], accum_out=den[:, c + j:c + j + 1]
                                         ).then_inc(achain, 1)
                nc.scalar.activation(es[:, c:c + 4], es[:, c:c + 4], ACT.Exp).then_inc(p_ready, 1)

            exps(0)
            for u, (n, g) in enumerate(units):
                act.wait_ge(pt_ready, u + 1)
                if u >= 2:
                    act.wait_ge(o_ready, u - 1)
                half = slice(1, 2) if n == 0 else slice(0, 2)
                nc.scalar.activation(PTH[:, u % 2, half], aux[0][:].rearrange("p (h j t) -> p h j t", h=2, j=4)[:, half],
                                     ACT.Copy).then_inc(pt_hi, 1)
                if u + 1 < len(units):
                    exps(u + 1)
                if u < 3:
                    split_q(u + 1)
                act.wait_ge(o_ready, u + 1)
                hp = slice(g * HD, (g + 1) * HD)
                nc.scalar.activation(AOH[hp, :, n * P:(n + 1) * P],
                                     aux[1][hp, 512 * (u % 2):512 * (u % 2 + 1)].rearrange("p (j t) -> p j t", j=4),
                                     ACT.Copy).then_inc(ao_hi, 1)

            for b in range(4):
                act.wait_ge(et_ready, b + 1)
                dst = (ETr, ETi)[b // 2]
                nc.scalar.activation(dst[:, (b % 2) * 8:(b % 2) * 8 + 8, :],
                                     (acc + aux)[b][:].rearrange("p (a t) -> p a t", a=8), ACT.Copy).then_inc(et_copied, 1)
            act.wait_ge(k_ready, 1)
            for h in range(2):
                nc.scalar.activation(Kt[:, 8 * h:8 * h + 8, :],
                                     halves_x[1][h][0:32, :].rearrange("p (a m) -> p a m", a=8), ACT.Copy
                                     ).then_inc(kt_copied, 1)

            def y_copy(b):
                act.wait_ge(yk_ready, b + 1)
                if b:
                    act.wait_ge(y_sb, b)
                nc.scalar.activation(Ysb[:, 8 * b:8 * b + 8, :].rearrange("p (a b) t -> p b a t", b=2),
                                     ybuf[b][:].rearrange("p (b a t) -> p b a t", b=2, a=4), ACT.Copy).then_inc(y_sb, 1)

            def gelu(t):
                act.wait_ge(z_in[t], 16)
                nc.scalar.activation(Z[:, t, :], Z[:, t, :], ACT.Gelu_apprx_tanh).then_inc(z_act, 1)
            y_copy(0)
            hi(START["glu"])
            gelu(0)
            y_copy(2)
            gelu(1)
            gelu(2)
            act.wait_ge(yk_ready, 4)
            for t in range(KW):
                if t == 3:
                    gelu(3)
                act.wait_ge(z_act, t + 1)
                nc.scalar.activation(ZH[:, t, :], Z[:, t, :], ACT.Copy).then_inc(zh_ready, 1)
            for t in range(KW):
                T = START["glu"] + t
                hi(T + 1)
                act.wait_ge(tile_done, T + 1)
                if t >= 2:
                    act.wait_ge(z2l, t - 1)
                nc.scalar.activation(S[:, t % 2, :], acc[T % 2][:], ACT.Sigmoid).then_inc(ev(T), 1)
                act.wait_ge(glu_mul, t + 1)
                nc.scalar.activation(perm(Z2H[:, t, :]), unperm(S[:, t % 2, :]), ACT.Copy).then_inc(z2h, 1)

            def merge1(i):
                for t in range(4):
                    T0 = START["merge1"] + t
                    hi_next(T0, 4, i)
                    if t >= 2:
                        act.wait_ge(m_sum, plus(t - 1, 2, i))
                        nc.scalar.activation(row(MH, plus(t - 2, 2, i)), S[:, t % 2, :], ACT.Copy).then_inc(mh_ready, 1)
            repeat(act, 4, merge1)
            for t in range(8):
                T = START["wout"] + t
                hi(T + 1)
                ev_wait(act, T)
                square(F, t, 1)
            hi(START["ff"] + 1)
            split_input(F, YH, g_pre2, x_scr[1], 1, 2)

            def ff(c):
                for t in range(12):
                    T0 = START["ff"] + t
                    if not (first_turn(c) and t == 0):
                        hi_next(T0, 12, c)
                    if t < 4:
                        act.wait_ge(tile_done, plus(T0 + 1, 12, c))
                        if t >= 2 or not first_turn(c):
                            act.wait_ge(hidden_lo, plus(t - 1, 4, c))
                        nc.scalar.activation(S[:, t % 2, :], acc[T0 % 2][:], ACT.Relu).then_inc(ev(T0), 1)
                        act.wait_ge(hidden_squared, plus(t + 1, 4, c))
                        nc.scalar.activation(HH[:, t, :], S[:, t % 2, :], ACT.Copy).then_inc(hidden_hi, 1)
                    elif isinstance(c, int) and c == FCH - 1:
                        act.wait_ge(f_final, t - 3)
                        if t == 4:
                            act.wait_ge(hidden_lo, 4 * FCH)
                        square(F, t - 4, 3)
            act.wait_ge(sq_added, 24)
            repeat(act, FCH, ff)
            hi(START["v2"] + 1)
            split_input(F, YH, g_pre3, x_scr[2], 2, 4)

            def v2_copy(t):
                act.wait_ge(vt2_ready, t + 1)
                nc.scalar.activation(V2[:, :, t * P:(t + 1) * P], aux[t % 2][:].rearrange("p (m n) -> p m n", m=MT),
                                     ACT.Copy).then_inc(v2_copied, 1)
            for t in range(4):
                T = START["v2"] + t
                if t != 0:
                    hi(T + 1)
                ev_wait(act, T)
                nc.scalar.activation(S[:, t % 2, :], S[:, t % 2, :], ACT.Gelu_apprx_tanh).then_inc(v2_gelu, 1)
                if t >= 1:
                    v2_copy(t - 1)
            hi(START["au"] + 1)
            v2_copy(3)
            act.wait_ge(ws_t, 1)
            nc.scalar.activation(wst[:], aux[0][:].rearrange("p (g t) -> p g t", g=8), ACT.Copy).then_inc(ws_c, 1)
            for t in range(8):
                T = START["au"] + t
                if t:
                    hi(T + 1)
                ev_wait(act, T)
                if t < 4:
                    nc.scalar.activation(Y[:, t, :], S[:, t % 2, :], ACT.Gelu_apprx_tanh).then_inc(a_gelu, 1)
                else:
                    if t >= 6:
                        act.wait_ge(a_product, t - 5)
                    nc.scalar.activation(Gb[t % 2][:], S[:, t % 2, :], ACT.Silu).then_inc(a_gelu, 1)
            for t in range(KW):
                act.wait_ge(sg_mul, t + 1)
                nc.scalar.activation(BH[:, t, :], S[:, t % 2, :], ACT.Copy).then_inc(branch_hi, 1)

            def merge2(stage, n, behind=None):
                def turn(i):
                    for t in range(4):
                        T0 = START[stage] + t
                        hi_next(T0, 4, i)
                        if t < 2:
                            ev_wait(act, T0, 4, i)
                            nc.scalar.activation(Gb[t][:], S[:, t, :], ACT.Sigmoid).then_inc(gate_made, 1)
                        if behind and isinstance(i, int) and i == 3:
                            behind(t)
                repeat(act, 4, turn)
            merge2("amerge", 0)
            for t in range(16):
                T = START["bx"] + t
                hi(T + 1)
                if t >= 12:
                    j = t - 12
                    ev_wait(act, T)
                    nc.scalar.activation(Gb[j % 2][:], S[:, j % 2, :], ACT.Silu).then_inc(b_silu, 1)
                    act.wait_ge(b_product, j + 1)
                    nc.scalar.activation(BH[:, j, :], Y[:, j, :], ACT.Copy).then_inc(branch_hi, 1)
            merge2("bmerge", 1)
            for t in range(12):
                T = START["cx"] + t
                hi(T + 1)
                if t < 4:
                    act.wait_ge(c_pooled, t + 1)
                    nc.scalar.activation(BH[:, t, :], Gb[t % 2][:], ACT.Copy).then_inc(branch_hi, 1)
                elif t < 8:
                    ev_wait(act, T)
                    nc.scalar.activation(Y[:, t - 4, :], S[:, t % 2, :], ACT.Silu).then_inc(c_silu, 1)
                else:
                    ev_wait(act, T)
                    nc.scalar.activation(BH[:, t - 8, :], S[:, t % 2, :], ACT.Copy).then_inc(branch_hi, 1)
            def split_m(f):
                act.wait_ge(m_added, 16 + f + 1)
                nc.scalar.activation(NHs[f // KW][:, f % KW, :], M[:, f, :], ACT.Copy).then_inc(m_hi, 1)

            def split_wo(i):
                p0 = NT // 2 + i
                act.wait_ge(w_in_s[p0 % 2], w_count(2 * p0))
                nc.scalar.activation(WOH[:, :, 256 * i:256 * (i + 1)], raw[:, p0 % 2], ACT.Copy).then_inc(wo_hi, 1)
            merge2("cmerge", 2, split_m)
            act.wait_ge(tile_done, NT - 2)
            split_wo(0)
            split_wo(1)
            act.wait_ge(tile_done, NT)
            for f in range(4, KD):
                split_m(f)
            split_wo(2)
            split_wo(3)
            for m in range(MT):
                act.wait_ge(ot_ready, m + 1)
                if m >= 1:
                    act.wait_ge(fsum, m)
                nc.scalar.activation(Gb[0][:], acc[m % 2][:], ACT.Square, accum_out=ss[:, m:m + 1]).then_inc(fsum, 1)

        @block.vector
        def _(dve):
            chain = [0]

            def link(ins):
                chain[0] += 1
                ins.then_inc(dchain, 1)
                dve.wait_ge(dchain, chain[0])

            TT, TS, STT = nc.vector.tensor_tensor, nc.vector.tensor_scalar, nc.vector.scalar_tensor_tensor

            def lo(T0, per=0, i=0):
                if T0 >= NT:
                    return
                dve.wait_ge(w_hi, plus(T0 + 1, per, i))
                kb = KOF[T0]
                TT(WL[:, T0 % 2, 0:kb, :], raw[:, (T0 // 2) % 2, 0:kb, (T0 % 2) * P:(T0 % 2 + 1) * P],
                   WH[:, T0 % 2, 0:kb, :].bitcast(f32), ALU.subtract).then_inc(w_lo, 1)

            def lo_next(T0, per, i):
                lo(T0 + 1 + per * i) if isinstance(i, int) else lo(T0 + 1, per, i)

            def done(T0, per=0, i=0):
                dve.wait_ge(tile_done, plus(T0 + 1, per, i))

            nc.vector.memset(one_col, 1.0 / D).then_inc(const_set, 1)
            nc.vector.memset(half_neg, -0.5).then_inc(const_set, 1)
            nc.vector.memset(ones[:], 1.0).then_inc(const_set, 1)
            for m in range(1, MT, 2):
                dve.wait_ge(xt_ready, m + 1)
                nc.vector.tensor_copy(XT[:, :, m * P:(m + 1) * P],
                                      aux[1][:].rearrange("p (k t) -> p k t", k=KD)).then_inc(xt_evicted_dve, 1)
            lo(0)
            dve.wait_ge(constants_loaded, 144)
            dve.wait_ge(id_in, 16)
            dve.wait_ge(xt_evicted_act, 4)
            dve.wait_ge(xt_evicted_dve, 4)

            def split_tile(src, dh, dl, gain, f, j):
                dve.wait_ge(xh_ready, 8 * j + f + 1)
                STT(dl[:, f, :], src[:, f, :], gain[:, f:f + 1], dh[:, f, :].bitcast(f32), ALU.mult, ALU.subtract
                    ).then_inc(xl_ready, 1)

            def rms_mean(n):
                dve.wait_ge(mean_ready, n + 1)
                TS(ms, aux[0][:, 0:KD], RMS_EPS, None, ALU.add).then_inc(ms_ready, 1)

            def rms_diag(n):
                dve.wait_ge(rtok_ready, n + 1)
                TT(ACC[:].rearrange("p (a b) -> p a b", a=MT),
                   ident[:].rearrange("p (o b) -> p o b", o=1).to_broadcast([P, MT, P]),
                   rtok.rearrange("p (a o) -> p a o", o=1).to_broadcast([P, MT, P]), ALU.mult).then_inc(rdg_ready, 1)

            def rms_spread(n, dst):
                dve.wait_ge(rb_ready, n + 1)
                link(nc.vector.tensor_copy(dst[:], aux[1][:]))

            def rms(n, dst):
                rms_mean(n)
                rms_diag(n)
                rms_spread(n, dst)

            def add_square(n, f):
                dve.wait_ge(sq_ready, 8 * n + f + 1)
                if f == 0:
                    nc.vector.tensor_copy(ACC[:], S[:, 0, :]).then_inc(sq_added, 1)
                else:
                    dve.wait_ge(sq_added, 8 * n + f)
                    TT(ACC[:], ACC[:], S[:, f % 2, :], ALU.add).then_inc(sq_added, 1)

            for f in range(KD):
                split_tile(XT, XH, XL, g_pre1, f, 0)
            lo(1)
            for f in range(KD):
                add_square(0, f)
            rms(0, RA)
            dve.wait_ge(x_out, 16 * 8)
            dve.wait_ge(sq_added, 8)
            dve.wait_ge(xl_ready, 8)
            for T in range(START["q"], START["gate1"]):
                if T:
                    lo(T + 1)
                done(T)
                TT(q[:, T, :] if T < 4 else k_[:] if T == 4 else S[:, 1, :], acc[T % 2][:], RA[:], ALU.mult
                   ).then_inc(ev(T), 1)

            def gates(i):
                for t in range(4):
                    T0 = START["gate1"] + t
                    lo_next(T0, 4, i)
                    done(T0, 4, i)
                    if t == 1 and first_turn(i):
                        dve.wait_ge(vt_ready, 1)
                    if t >= 2 or not first_turn(i):
                        dve.wait_ge(gate_ready, plus(t - 1, 4, i))
                    TT(S[:, t % 2, :], acc[T0 % 2][:], RA[:], ALU.mult).then_inc(ev(T0), 1)
            repeat(dve, 4, gates)
            for t in range(4):
                T = START["u"] + t
                if t < 3:
                    lo(T + 1)
                if t == 1:
                    dve.wait_ge(kv_hi, 2)
                    TT(KL[:], k_[:], KH[:].bitcast(f32), ALU.subtract).then_inc(kv_lo, 1)
                    TT(VL[:], v[:], VH[:].bitcast(f32), ALU.subtract).then_inc(kv_lo, 1)
                    dve.wait_ge(ct_ready, 8)
                    for b in range(4):
                        for g2 in range(2):
                            pp = slice(g2 * NS, (g2 + 1) * NS)
                            re, im = (aux[n][:].rearrange("p (t a b c) -> p t a b c", t=8, a=4, b=2)[pp, b, :, g2, :]
                                      for n in range(2))
                            nc.vector.tensor_copy(Cr[pp, 4 * b:4 * b + 4, :], re).then_inc(c_ready, 1)
                            TS(nCi[pp, 4 * b:4 * b + 4, :], im, -1.0, None, ALU.mult).then_inc(c_ready, 1)
                done(T)
                if t >= 2:
                    dve.wait_ge(u_out[t % 2], 16)
                TT(unperm(ust[:, t % 2, :]), perm(acc[T % 2][:]), perm(RA[:]), ALU.mult).then_inc(ev(T), 1)

            units = [(n, g) for n in range(MT) for g in range(KV)]

            def split_q(c):
                sl = slice(256 * c, 256 * (c + 1))
                dve.wait_ge(q_hi, c + 1)
                TT(QL[:, :, sl], q[:, :, sl], QH[:, :, sl].bitcast(f32), ALU.subtract).then_inc(q_lo, 1)
            split_q(0)
            dve.wait_ge(b_in, 16)

            def soft(u):
                n, g = units[u]
                lo_ = P if n == 0 else 0
                c = 4 * (u % 2)
                dve.wait_ge(s_ready, u + 1)
                if u >= 2:
                    dve.wait_ge(pt_ready, u - 1)
                L = prob[:, u % 2, :, lo_:]
                STT(L, acc[u % 2][:].rearrange("p (j s) -> p j s", j=4)[:, :, lo_:], HD ** -0.5,
                    bias[:, 4 * g:4 * g + 4, lo_:], ALU.mult, ALU.add).then_inc(s_read, 1)
                dve.wait_ge(s_read, u + 1)
                link(nc.vector.reduce_max(mx[:, c:c + 4], L, AX.X))
                link(TT(mx[:, c:c + 4], mx[:, c:c + 4], sink[:, 4 * g:4 * g + 4], ALU.max))
                link(TS(nm[:, c:c + 4], mx[:, c:c + 4], -1.0, None, ALU.mult))
                TT(es[:, c:c + 4], sink[:, 4 * g:4 * g + 4], mx[:, c:c + 4], ALU.subtract).then_inc(nm_ready, 1)

            def normalise(u):
                n, g = units[u]
                lo_ = P if n == 0 else 0
                c = 4 * (u % 2)
                dve.wait_ge(p_ready, u + 1)
                link(TT(den[:, c:c + 4], den[:, c:c + 4], es[:, c:c + 4], ALU.add))
                link(nc.vector.reciprocal(rd[:, c:c + 4], den[:, c:c + 4]))
                L = prob[:, u % 2, :, lo_:]
                TT(L, L, rd[:, c:c + 4].rearrange("p (j o) -> p j o", o=1).to_broadcast([P, 4, 2 * P - lo_]), ALU.mult
                   ).then_inc(pn_ready, 1)
            soft(0)
            soft(1)
            normalise(0)
            for u, (n, g) in enumerate(units):
                dve.wait_ge(pt_hi, u + 1)
                half = slice(1, 2) if n == 0 else slice(0, 2)
                TT(PTL[:, u % 2, half], aux[0][:].rearrange("p (h j t) -> p h j t", h=2, j=4)[:, half],
                   PTH[:, u % 2, half].bitcast(f32), ALU.subtract).then_inc(pt_lo, 1)
                if u + 1 < len(units):
                    normalise(u + 1)
                if u < 3:
                    split_q(u + 1)
                if u + 2 < len(units):
                    soft(u + 2)
                dve.wait_ge(ao_hi, u + 1)
                hp, sl = slice(g * HD, (g + 1) * HD), slice(n * P, (n + 1) * P)
                TT(AOL[hp, :, sl], aux[1][hp, 512 * (u % 2):512 * (u % 2 + 1)].rearrange("p (j t) -> p j t", j=4),
                   AOH[hp, :, sl].bitcast(f32), ALU.subtract).then_inc(ao_lo, 1)

            dve.wait_ge(rot_ready, 1)
            dve.wait_ge(o_ready, 16)
            link(nc.vector.tensor_copy(Dk[:], lam[:, 19, :].rearrange("p (a o) -> p a o", o=1).to_broadcast([P, PAIRS, CH])))
            link(nc.vector.memset(Dk[:, :, 0:1], 0.0))
            flat = lambda t: t[:].rearrange("p a h -> p (a h)")
            a, b = slice(1, CH), slice(0, CH - 1)
            for h in range(2):
                sl, pr = slice(1024 * h, 1024 * (h + 1)), slice(8 * h, 8 * h + 8)
                dve.wait_ge(x_ready, h + 1)
                xr_, xi_ = halves_x[h][0][:], halves_x[h][1][:]
                link(TT(S[:, 0, :], xr_, flat(RC)[:, sl], ALU.mult))
                link(TT(S[:, 1, :], xi_, flat(RS)[:, sl], ALU.mult))
                link(TT(flat(Vr)[:, sl], S[:, 0, :], S[:, 1, :], ALU.add))
                link(TT(S[:, 0, :], xi_, flat(RC)[:, sl], ALU.mult))
                link(TT(S[:, 1, :], xr_, flat(RS)[:, sl], ALU.mult))
                link(TT(flat(Vi)[:, sl], S[:, 0, :], S[:, 1, :], ALU.subtract))
                for t in (Vr, Vi):
                    link(nc.vector.tensor_tensor_scan(flat(t)[:, sl], flat(Dk)[:, sl], flat(t)[:, sl], 0.0,
                                                      ALU.mult, ALU.add))
                link(nc.vector.memset(Hr[:, pr, 0:1], 0.0))
                link(nc.vector.memset(Hi[:, pr, 0:1], 0.0))
                link(TT(Hr[:, pr, a], Vr[:, pr, b], RC[:, pr, b], ALU.mult))
                link(TT(Dk[:, pr, b], Vi[:, pr, b], RS[:, pr, b], ALU.mult))
                link(TT(Hr[:, pr, a], Hr[:, pr, a], Dk[:, pr, b], ALU.subtract))
                link(TT(Hi[:, pr, a], Vr[:, pr, b], RS[:, pr, b], ALU.mult))
                link(TT(Dk[:, pr, b], Vi[:, pr, b], RC[:, pr, b], ALU.mult))
                TT(Hi[:, pr, a], Hi[:, pr, a], Dk[:, pr, b], ALU.add).then_inc(h_ready, 1)
            for n in (1, 3):
                dve.wait_ge(yk_ready, n + 1)
                dve.wait_ge(y_sb, n)
                nc.vector.tensor_copy(Ysb[:, 8 * n:8 * n + 8, :].rearrange("p (a b) t -> p b a t", b=2),
                                      ybuf[n][:].rearrange("p (b a t) -> p b a t", b=2, a=4)).then_inc(y_sb, 1)
            lo(START["glu"])
            for t in range(KW):
                dve.wait_ge(zh_ready, t + 1)
                TT(ZL[:, t, :], Z[:, t, :], ZH[:, t, :].bitcast(f32), ALU.subtract).then_inc(zl_ready, 1)
            for t in range(KW):
                T = START["glu"] + t
                lo(T + 1)
                ev_wait(dve, T)
                TT(S[:, t % 2, :], S[:, t % 2, :], Z[:, t, :], ALU.mult).then_inc(glu_mul, 1)
                dve.wait_ge(z2h, t + 1)
                TT(perm(Z2L[:, t, :]), unperm(S[:, t % 2, :]), perm(Z2H[:, t, :]).bitcast(f32), ALU.subtract
                   ).then_inc(z2l, 1)
            dve.wait_ge(z2l, 4)

            def merge1(i):
                for t in range(4):
                    T0 = START["merge1"] + t
                    lo_next(T0, 4, i)
                    done(T0, 4, i)
                    dve.wait_ge(ga_in[t], plus(16, 16, i))
                    if t < 2:
                        if not first_turn(i):
                            dve.wait_ge(ml_ready, plus(t - 1, 2, i))
                        TT(S[:, t, :], acc[T0 % 2][:], gin[:, t, :], ALU.mult).then_inc(ev(T0), 1)
                    else:
                        if not first_turn(i):
                            dve.wait_ge(m_sum, plus(t - 3, 2, i))
                        gt = (ACC, RP)[t % 2]
                        TT(gt[:], acc[T0 % 2][:], gin[:, t, :], ALU.mult).then_inc(ev(T0), 1)
                        ev_wait(dve, T0, 4, i)
                        ev_wait(dve, T0 - 2, 4, i)
                        TT(S[:, t % 2, :], S[:, t % 2, :], gt[:], ALU.add).then_inc(m_sum, 1)
                        dve.wait_ge(mh_ready, plus(t - 1, 2, i))
                        f = plus(t - 2, 2, i)
                        TT(row(ML, f), S[:, t % 2, :], row(MH, f).bitcast(f32), ALU.subtract).then_inc(ml_ready, 1)
            repeat(dve, 4, merge1)
            for t in range(8):
                T = START["wout"] + t
                lo(T + 1)
                done(T)
                nc.vector.tensor_copy(F[:, t, :], acc[T % 2][:]).then_inc(ev(T), 1)
                if t == 0:
                    dve.wait_ge(rb_ready, 1)
                if t:
                    add_square(1, t - 1)
            add_square(1, 7)

            def post_norm(n, j, gpost, gpre):
                rms(n, RP)
                for f in range(KD + 1):
                    if f < KD:
                        STT(F[:, f, :], F[:, f, :], gpost[:, f:f + 1], RP[:], ALU.mult, ALU.mult).then_inc(f_scaled, 1)
                    if f >= 1:
                        split_tile(F, YH, YL, gpre, f - 1, j)
                    if f < KD:
                        dve.wait_ge(f_scaled, 8 * (j - 1) + f + 1)
                        dve.wait_ge(xr_in[f % 3], 16 * ((j - 1) * (2 if f % 3 == 2 else 3) + f // 3 + 1))
                        TT(F[:, f, :], F[:, f, :], (xr1, xr2)[j - 1][:, f % 3, :], ALU.add).then_inc(x_added, 1)
            ev_wait(dve, START["wout"] + 6)
            ev_wait(dve, START["wout"] + 7)
            lo(START["ff"] + 1)
            post_norm(1, 1, g_post1, g_pre2)

            def ff(c):
                for t in range(12):
                    T0 = START["ff"] + t
                    if not (first_turn(c) and t == 0):
                        lo_next(T0, 12, c)
                    done(T0, 12, c)
                    if t < 4:
                        ev_wait(dve, T0, 12, c)
                        TT(S[:, t % 2, :], S[:, t % 2, :], S[:, t % 2, :], ALU.mult).then_inc(hidden_squared, 1)
                        dve.wait_ge(hidden_hi, plus(t + 1, 4, c))
                        TT(HL[:, t, :], S[:, t % 2, :], HH[:, t, :].bitcast(f32), ALU.subtract).then_inc(hidden_lo, 1)
                    else:
                        f = t - 4
                        if first_turn(c):
                            dve.wait_ge(f_zero, 1)
                        ev_wait(dve, T0 - 12, 12, c)
                        TT(F[:, f, :], F[:, f, :], acc[T0 % 2][:], ALU.add).then_inc(ev(T0), 1)
                        if first_turn(c) and t == 4:
                            rms_mean(2)
                        if first_turn(c) and t == 5:
                            rms_diag(2)
                        if first_turn(c) and t == 6:
                            rms_spread(2, RA)
                            link(TT(RA[:], RA[:], RA[:], ALU.mult))
                        if isinstance(c, int) and c == FCH - 1:
                            ev_wait(dve, T0, 12, c)
                            TT(F[:, f, :], F[:, f, :], RA[:], ALU.mult).then_inc(f_final, 1)
                            if f:
                                add_square(3, f - 1)
            repeat(dve, FCH, ff)
            add_square(3, 7)
            dve.wait_ge(f_final, 8)
            lo(START["v2"] + 1)
            post_norm(3, 2, g_post2, g_pre3)
            rms(4, RA)

            dve.wait_ge(xl_ready, 24)
            dve.wait_ge(x_out, 16 * 24)
            dve.wait_ge(sq_added, 40)
            for t in range(4):
                T = START["v2"] + t
                if t:
                    lo(T + 1)
                done(T)
                if t >= 2:
                    dve.wait_ge(vt2_ready, t - 1)
                TT(S[:, t % 2, :], acc[T % 2][:], RA[:], ALU.mult).then_inc(ev(T), 1)
            dve.wait_ge(block2_loaded, 16 * 6)
            for t in range(8):
                T = START["au"] + t
                lo(T + 1)
                vt = V2[:, t, :]
                dve.wait_ge(v2_copied, 4)
                link(nc.vector.bn_stats(bn, vt))
                link(nc.vector.bn_aggr(ag, bn))
                TS(lnv, ag[:, 1:2], LN_EPS, None, ALU.add).then_inc(ln_var, 1)
                dve.wait_ge(ln_r, t + 1)
                link(TS(vt, vt, ag[:, 0:1], lnr, ALU.subtract, ALU.mult))
                link(TT(vt, vt, lng[:], ALU.mult))
                TT(vt, vt, lnb[:], ALU.add).then_inc(ln_done, 1)
                done(T)
                if t < 2:
                    dve.wait_ge(vt2_ready, t + 3)
                else:
                    dve.wait_ge(a_gelu, t - 1)
                TT(S[:, t % 2, :], acc[T % 2][:], RA[:], ALU.mult).then_inc(ev(T), 1)
                if t >= 4:
                    dve.wait_ge(a_gelu, t + 1)
                    TT(Y[:, t - 4, :], Y[:, t - 4, :], Gb[t % 2][:], ALU.mult).then_inc(a_product, 1)
            for t in range(KW):
                dve.wait_ge(sg_ready, t + 1)
                dve.wait_ge(a_gelu, 8)
                if t >= 2:
                    dve.wait_ge(branch_lo, t - 1)
                TT(S[:, t % 2, :].rearrange("p (n t) -> p n t", n=MT), aux[t % 2][:].rearrange("p (n t) -> p n t", n=MT),
                   bsb[:, t:t + 1, :].to_broadcast([P, MT, P]), ALU.add).then_inc(sg_add, 1)
                dve.wait_ge(sg_add, t + 1)
                dve.wait_ge(a_product, t + 1)
                TT(S[:, t % 2, :], S[:, t % 2, :], Y[:, t, :], ALU.mult).then_inc(sg_mul, 1)
                dve.wait_ge(branch_hi, t + 1)
                TT(BL[:, t, :], S[:, t % 2, :], BH[:, t, :].bitcast(f32), ALU.subtract).then_inc(branch_lo, 1)

            def merge2(stage, n, ahead=None, behind=None):
                def turn(i):
                    for t in range(4):
                        T0 = START[stage] + t
                        lo_next(T0, 4, i)
                        last_turn = isinstance(i, int) and i == 3
                        if ahead and last_turn and t == 3:
                            ahead(0)
                        done(T0, 4, i)
                        if t < 2:
                            if not first_turn(i):
                                dve.wait_ge(m_added, plus(8 * n + t - 1, 2, i))
                            TT(S[:, t, :], acc[T0 % 2][:], RA[:], ALU.mult).then_inc(ev(T0), 1)
                        else:
                            dve.wait_ge(gate_made, plus(8 * n + t - 1, 2, i))
                            TT(S[:, t % 2, :], acc[T0 % 2][:], Gb[t % 2][:], ALU.mult).then_inc(ev(T0), 1)
                        if behind and last_turn:
                            behind(t)
                repeat(dve, 4, turn)
                dve.wait_ge(m_added, 8 * (n + 1))
            dve.wait_ge(branch_lo, 4)
            merge2("amerge", 0)
            for t in range(16):
                T = START["bx"] + t
                j = t % 4
                lo(T + 1)
                done(T)
                if t < 4:
                    TT(Y[:, j, :], acc[T % 2][:], RA[:], ALU.mult).then_inc(ev(T), 1)
                elif t < 8:
                    Gj, Yj = Gb[j % 2], Y[:, j, :]
                    if j >= 2:
                        dve.wait_ge(b_convolved, j - 1)
                    ev_wait(dve, START["bx"] + j)
                    TT(Gj[:], acc[T % 2][:], RA[:], ALU.mult).then_inc(ev(T), 1)
                    ev_wait(dve, T)
                    link(TT(Gj[:], Gj[:], Yj, ALU.mult))
                    link(TS(Yj, Gj[:], cw[:, 2 * KW + j:2 * KW + j + 1], cb[:, j:j + 1], ALU.mult, ALU.add))
                    link(STT(Yj[:, 1:], Gj[:, :SEQ - 1], cw[:, KW + j:KW + j + 1], Yj[:, 1:], ALU.mult, ALU.add))
                    STT(Yj[:, 2:], Gj[:, :SEQ - 2], cw[:, j:j + 1], Yj[:, 2:], ALU.mult, ALU.add).then_inc(b_convolved, 1)
                elif t < 12:
                    dve.wait_ge(b_convolved, j + 1)
                    if j >= 2:
                        dve.wait_ge(b_gated, j - 1)
                    TT(S[:, j % 2, :], acc[T % 2][:], RA[:], ALU.mult).then_inc(ev(T), 1)
                    ev_wait(dve, T)
                    TT(Y[:, j, :], Y[:, j, :], S[:, j % 2, :], ALU.mult).then_inc(b_gated, 1)
                else:
                    dve.wait_ge(b_gated, 4)
                    if j >= 2:
                        dve.wait_ge(b_silu, j - 1)
                    TT(S[:, j % 2, :], acc[T % 2][:], RA[:], ALU.mult).then_inc(ev(T), 1)
                    dve.wait_ge(b_silu, j + 1)
                    TT(Y[:, j, :], Y[:, j, :], Gb[j % 2][:], ALU.mult).then_inc(b_product, 1)
                    dve.wait_ge(branch_hi, 4 + j + 1)
                    TT(BL[:, j, :], Y[:, j, :], BH[:, j, :].bitcast(f32), ALU.subtract).then_inc(branch_lo, 1)
            merge2("bmerge", 1)
            for t in range(12):
                T = START["cx"] + t
                j = t % 4
                lo(T + 1)
                done(T)
                if t < 4:
                    w = POOLS[j]
                    X0 = Y[:, j, :]
                    TT(X0, acc[T % 2][:], RA[:], ALU.mult).then_inc(ev(T), 1)
                    ev_wait(dve, T)
                    if t >= 1:
                        dve.wait_ge(branch_lo, 8 + t)
                    if t == 0:
                        dve.wait_ge(branch_lo, 8)
                    src, shift, n = X0, 1, 0
                    while shift < w:
                        dst = S[:, n % 2, :]
                        link(TT(dst[:, shift:], src[:, shift:], src[:, :SEQ - shift], ALU.add))
                        link(nc.vector.tensor_copy(dst[:, :shift], src[:, :shift]))
                        src, shift, n = dst, 2 * shift, n + 1
                    link(TT(src[:, 0:16], src[:, 0:16], cnt[:, j, :], ALU.mult))
                    STT(Gb[j % 2][:], src, 1.0 / w, X0, ALU.mult, ALU.subtract).then_inc(c_pooled, 1)
                    dve.wait_ge(branch_hi, 8 + j + 1)
                    TT(BL[:, j, :], Gb[j % 2][:], BH[:, j, :].bitcast(f32), ALU.subtract).then_inc(branch_lo, 1)
                elif t < 8:
                    if t == 4:
                        dve.wait_ge(branch_lo, 12)
                    if j >= 2:
                        dve.wait_ge(c_silu, j - 1)
                    TT(S[:, t % 2, :], acc[T % 2][:], RA[:], ALU.mult).then_inc(ev(T), 1)
                else:
                    dve.wait_ge(c_silu, 4)
                    if j >= 2:
                        dve.wait_ge(branch_lo, 12 + j - 1)
                    STT(S[:, t % 2, :], acc[T % 2][:], psc[:, j:j + 1], Y[:, j, :], ALU.mult, ALU.mult).then_inc(ev(T), 1)
                    dve.wait_ge(branch_hi, 12 + j + 1)
                    TT(BL[:, j, :], S[:, t % 2, :], BH[:, j, :].bitcast(f32), ALU.subtract).then_inc(branch_lo, 1)
            dve.wait_ge(branch_lo, 16)
            def split_m(f):
                dve.wait_ge(m_hi, f + 1)
                TT(NL[:, f, :], M[:, f, :], NHs[f // KW][:, f % KW, :].bitcast(f32), ALU.subtract).then_inc(m_lo, 1)

            def split_wo(i):
                dve.wait_ge(wo_hi, i + 1)
                TT(WOL[:, :, 256 * i:256 * (i + 1)], raw[:, (NT // 2 + i) % 2],
                   WOH[:, :, 256 * i:256 * (i + 1)].bitcast(f32), ALU.subtract).then_inc(wo_lo, 1)
            merge2("cmerge", 2, split_wo, split_m)
            split_wo(1)
            for f in range(4, KD):
                split_m(f)
            split_wo(2)
            split_wo(3)
            dve.wait_ge(fg_loaded, 16)
            for m in range(MT):
                dve.wait_ge(fsum, m + 1)
                TS(fv[:, m:m + 1], ss[:, m:m + 1], 1.0 / D, RMS_EPS, ALU.mult, ALU.add).then_inc(fv_r, 1)
                dve.wait_ge(fr_r, m + 1)
                if m >= 2:
                    dve.wait_ge(stored[m % 2], 16 * (m // 2))
                STT(S[:, m % 2, :], acc[m % 2][:], fr[:, m:m + 1], fgb[:], ALU.mult, ALU.mult).then_inc(o_done, 1)

        @block.tensor
        def _(pe):
            mm = nc.tensor.matmul

            def begin(T0, per, i):
                pe.wait_ge(w_lo, plus(T0 + 1, per, i))
                if T0 >= 2:
                    pe.wait_ge(evicted[T0 % 2], plus(T0 // 2, per // 2, i))

            def w_tile(T0, xh, xl, per=0, i=0, each=None):
                begin(T0, per, i)
                kb, a, s_ = KOF[T0], acc[T0 % 2], T0 % 2
                for k in range(kb):
                    if each:
                        each(k)
                    for w, x in ((WH, xh), (WH, xl), (WL, xh)):
                        for h in range(2):
                            sl = slice(512 * h, 512 * (h + 1))
                            last = mm(a[:, sl], w[:, s_, k, :], x[:, k, sl], start=(k == 0 and w is WH and x is xh),
                                      stop=(k == kb - 1 and w is WL))
                last.then_inc(tile_done, 1)

            def norm_mean(n):
                pe.wait_ge(sq_added, 8 * (n + 1))
                for m in range(MT):
                    last = mm(aux[0][:, m:m + 1], ACC[:, m * P:(m + 1) * P], one_col, start=True, stop=True)
                last.then_inc(mean_ready, 1)

            def norm_spread(n):
                pe.wait_ge(rdg_ready, n + 1)
                for h in range(2):
                    sl = slice(512 * h, 512 * (h + 1))
                    last = mm(aux[1][:, sl], ones[:], ACC[:, sl], start=True, stop=True)
                last.then_inc(rb_ready, 1)

            pe.wait_ge(id_in, 16)
            for m in range(MT):
                pe.wait_ge(x_in[m], 16)
                if m >= 2:
                    pe.wait_ge((xt_evicted_act, xt_evicted_dve)[m % 2], m // 2)
                for k in range(KD):
                    last = nc.tensor.transpose(aux[m % 2][:, k * P:(k + 1) * P], xtok[:, m, k * P:(k + 1) * P], ident[:])
                last.then_inc(xt_ready, 1)
            pe.wait_ge(bs_in, 32)
            pe.wait_ge(ones_set, 1)
            pe.wait_ge(xt_evicted_dve, 4)
            mm(aux[1][0:HEADS, 0:ROWLEN], rel[:], bsel[:], start=True, stop=True).then_inc(b_row, 1)
            pe.wait_ge(const_set, 3)
            pe.wait_ge(b_rowsb, 1)
            pe.wait_ge(xt_evicted_act, 4)
            w_tile(0, XH, XL, each=lambda k: pe.wait_ge(xl_ready, k + 1))
            w_tile(1, XH, XL)
            norm_mean(0)
            norm_spread(0)
            for T in range(2, START["gate1"]):
                w_tile(T, XH, XL)

            def gates(i):
                for t in range(4):
                    w_tile(START["gate1"] + t, XH, XL, 4, i)
                    if t == 0 and first_turn(i):
                        ev_wait(pe, START["kv"] + 1)
                        for m in range(MT):
                            last = nc.tensor.transpose(aux[0][:, m * P:(m + 1) * P], S[:, 1, m * P:(m + 1) * P], ident[:])
                        last.then_inc(vt_ready, 1)
            repeat(pe, 4, gates)
            pe.wait_ge(v_copied, 1)
            pe.wait_ge(ssm_loaded, 16 * 17)
            for n in range(2):
                for t in range(4):
                    nc.tensor.transpose(aux[n][:, t * P:(t + 1) * P], Cn[:, n, t].rearrange("p a s -> p (a s)"), ident[:]
                                        ).then_inc(ct_ready, 1)
            for t in range(4):
                w_tile(START["u"] + t, XH, XL)

            units = [(n, g) for n in range(MT) for g in range(KV)]
            ev_wait(pe, START["u"] + 2)
            ev_wait(pe, START["u"] + 3)
            pe.wait_ge(c_ready, 16)
            pe.wait_ge(kv_lo, 2)

            def scores(u):
                n, g = units[u]
                lo_ = P if n == 0 else 0
                if u >= 2:
                    pe.wait_ge(s_read, u - 1)
                pe.wait_ge(q_lo, n // 2 + 1)
                hp, tq, tk = slice(g * HD, (g + 1) * HD), slice(n * P, (n + 1) * P), slice((n - 1) * P + lo_, (n + 1) * P)
                for j in range(4):
                    for a, b in ((QH, KH), (QH, KL), (QL, KH)):
                        last = mm(acc[u % 2][:, j * 256 + lo_:(j + 1) * 256], a[hp, j, tq], b[hp, tk],
                                  start=(a is QH and b is KH), stop=(a is QL))
                last.then_inc(s_ready, 1)
            scores(0)
            scores(1)
            for u, (n, g) in enumerate(units):
                pe.wait_ge(pn_ready, u + 1)
                if u >= 1:
                    pe.wait_ge(pt_lo, u)
                halves = (1,) if n == 0 else (0, 1)
                for h in halves:
                    for j in range(4):
                        b = (4 * h + j) * P
                        last = nc.tensor.transpose(aux[0][:, b:b + P], prob[:, u % 2, j, h * P:(h + 1) * P], ident[:])
                last.then_inc(pt_ready, 1)
                if u + 2 < len(units):
                    scores(u + 2)
                pe.wait_ge(pt_lo, u + 1)
                if u >= 2:
                    pe.wait_ge(ao_lo, u - 1)
                for h in halves:
                    for a, b in ((VH, PTH), (VH, PTL), (VL, PTH)):
                        last = mm(aux[1][:, 512 * (u % 2):512 * (u % 2 + 1)], a[:, n - 1 + h, :],
                                  b[:, u % 2, h].rearrange("p j t -> p (j t)"),
                                  start=(h == halves[0] and a is VH and b is PTH), stop=(h == 1 and a is VL))
                last.then_inc(o_ready, 1)

            pe.wait_ge(ao_lo, 16)
            pe.wait_ge(m1_ready, 1)
            for b in range(4):
                src = (M1r, M1i)[b // 2]
                for a in range(8):
                    last = nc.tensor.transpose((acc + aux)[b][:, a * P:(a + 1) * P],
                                               src[:, (b % 2) * 8 + a].rearrange("p t c -> p (t c)"), ident[:])
                last.then_inc(et_ready, 1)
            def chunk_inputs(h):
                for a in range(8):
                    for g2 in range(2):
                        pp = slice(g2 * NS, (g2 + 1) * NS)
                        for dst, e in zip(halves_x[h], (ETr, ETi)):
                            last = mm(dst[pp, a * P:(a + 1) * P], e[:, 8 * h + a, pp], U[:, 2 * (8 * h + a) + g2, :],
                                      start=True, stop=True)
                last.then_inc(x_ready, 1)
            pe.wait_ge(u_in, 16 * TAU)
            pe.wait_ge(et_copied, 4)
            chunk_inputs(0)
            for a in range(PAIRS):
                dst = halves_x[1][a // 8][0:32, (a % 8) * P:(a % 8 + 1) * P]
                mm(dst, BBr[:, a].rearrange("p b c -> p (b c)"), FXr[:, a, 0:TAU].rearrange("p t c -> p (t c)"),
                   start=True, stop=False)
                last = mm(dst, BBi[:, a].rearrange("p b c -> p (b c)"), FXi[:, a, 0:TAU].rearrange("p t c -> p (t c)"),
                          start=False, stop=True)
            last.then_inc(k_ready, 1)
            pe.wait_ge(kt_copied, 2)
            chunk_inputs(1)
            pe.wait_ge(l_in, 16 * 16)
            for b in range(4):
                pe.wait_ge(h_ready, b // 2 + 1)
                buf = ybuf[b]
                for a in range(4):
                    pr = 4 * b + a
                    for g2 in range(2):
                        pp = slice(g2 * NS, (g2 + 1) * NS)
                        dst = buf[:, g2 * 512 + a * P:g2 * 512 + (a + 1) * P]
                        mm(dst, Lm[:, 2 * pr + g2, :], U[:, 2 * pr + g2, :], start=True, stop=False)
                        mm(dst, FXr[pp, pr, 1:].rearrange("p t c -> p (t c)"), Hr[pp, pr, :], start=False, stop=False)
                        last = mm(dst, FXi[pp, pr, 1:].rearrange("p t c -> p (t c)"), Hi[pp, pr, :], start=False, stop=True)
                last.then_inc(yk_ready, 1)
            pe.wait_ge(y_sb, 3)
            w_tile(START["glu"], ZH, ZL, each=lambda k: pe.wait_ge(zl_ready, k + 1))
            for t in range(1, 4):
                w_tile(START["glu"] + t, ZH, ZL)

            def merge1(i):
                for t in range(4):
                    if t == 2 and first_turn(i):
                        pe.wait_ge(z2l, 4)
                    w_tile(START["merge1"] + t, (AOH, Z2H)[t // 2], (AOL, Z2L)[t // 2], 4, i)
            repeat(pe, 4, merge1)
            w_tile(START["wout"], MH, ML, each=lambda k: pe.wait_ge(ml_ready, k + 1))
            for t in range(1, 8):
                w_tile(START["wout"] + t, MH, ML)
            norm_mean(1)
            norm_spread(1)

            def ff(c):
                for t in range(4):
                    w_tile(START["ff"] + t, YH, YL, 12, c, each=(lambda k: pe.wait_ge(xl_ready, 8 + k + 1))
                           if t == 0 and first_turn(c) else None)
                for t in range(4, 12):
                    w_tile(START["ff"] + t, HH, HL, 12, c,
                           each=(lambda k: pe.wait_ge(hidden_lo, plus(k + 1, 4, c))) if t == 4 else None)
                    if first_turn(c) and t == 4:
                        norm_mean(2)
                    if first_turn(c) and t == 6:
                        norm_spread(2)
            repeat(pe, FCH, ff)
            norm_mean(3)
            norm_spread(3)

            def v2_transpose(t):
                pe.wait_ge(v2_gelu, t + 1)
                if t >= 2:
                    pe.wait_ge(v2_copied, t - 1)
                for m in range(MT):
                    last = nc.tensor.transpose(aux[t % 2][:, m * P:(m + 1) * P], S[:, t % 2, m * P:(m + 1) * P], ident[:])
                last.then_inc(vt2_ready, 1)
            w_tile(START["v2"], YH, YL, each=lambda k: pe.wait_ge(xl_ready, 16 + k + 1))
            w_tile(START["v2"] + 1, YH, YL)
            norm_mean(4)
            norm_spread(4)
            w_tile(START["v2"] + 2, YH, YL)
            v2_transpose(0)
            w_tile(START["v2"] + 3, YH, YL)
            v2_transpose(1)
            v2_transpose(2)
            w_tile(START["au"], YH, YL)
            v2_transpose(3)
            pe.wait_ge(v2_copied, 3)
            pe.wait_ge(block2_loaded, 16 * 6)
            for g in range(8):
                last = nc.tensor.transpose(aux[0][:, g * P:(g + 1) * P], wsr[:, g, :], ident[:])
            last.then_inc(ws_t, 1)
            for t in range(1, 8):
                w_tile(START["au"] + t, YH, YL)
            pe.wait_ge(ln_done, MT)
            pe.wait_ge(v2_copied, 4)
            pe.wait_ge(ws_m, 1)
            for t in range(KW):
                if t >= 2:
                    pe.wait_ge(sg_add, t - 1)
                for n in range(MT):
                    for h in range(2):
                        g = 2 * t + h
                        last = mm(aux[t % 2][h * 64:(h + 1) * 64, n * P:(n + 1) * P], V2[:, n, g * 64:(g + 1) * 64],
                                  wst[:, g, :], start=True, stop=True)
                last.then_inc(sg_ready, 1)

            def merge2(stage, n):
                def turn(i):
                    for t in range(4):
                        w_tile(START[stage] + t, (YH, BH)[t // 2], (YL, BL)[t // 2], 4, i,
                               each=(lambda k: pe.wait_ge(branch_lo, n + k + 1)) if t == 2 and first_turn(i) else None)
                repeat(pe, 4, turn)
            merge2("amerge", 0)
            for t in range(16):
                w_tile(START["bx"] + t, YH, YL)
            merge2("bmerge", 4)
            for t in range(8):
                w_tile(START["cx"] + t, YH, YL)
            for t in range(4):
                pe.wait_ge(branch_lo, 12)
                w_tile(START["pool"] + t, BH[:, t:t + 1, :], BL[:, t:t + 1, :])
            merge2("cmerge", 12)
            ev_wait(pe, NT - 2)
            ev_wait(pe, NT - 1)
            for m in range(MT):
                if m >= 2:
                    pe.wait_ge(o_done, m - 1)
                tk = slice(m * P, (m + 1) * P)
                for h in range(2):
                    sl = slice(512 * h, 512 * (h + 1))
                    if m == 0:
                        pe.wait_ge(wo_lo, 2 * h + 2)
                    for k in range(KD):
                        if m == 0 and h == 0:
                            pe.wait_ge(m_lo, k + 1)
                        nh_k, nl_k = NHs[k // KW][:, k % KW, tk], NL[:, k, tk]
                        for n, (x, w) in enumerate(((nh_k, WOH), (nh_k, WOL), (nl_k, WOH))):
                            last = mm(acc[m % 2][:, sl], x, w[:, k, sl], start=(k == 0 and n == 0),
                                      stop=(k == KD - 1 and n == 2))
                        if k == KD - 2:
                            if h == 0:
                                pe.wait_ge(x3_in[m % 3], 16 * (m // 3 + 1))
                            for f in range(4 * h, 4 * h + 4):
                                mm(acc[m % 2][:, f * P:(f + 1) * P], xr3[:, m % 3, f, :], ident[:], start=False, stop=False)
                last.then_inc(ot_ready, 1)

        @block.gpsimd
        def _(pool):
            TT = nc.gpsimd.tensor_tensor
            nc.gpsimd.memset(rel[BUCKETS:BUCKETS + 1, :], NEG).then_inc(ones_set, 1)

            def add_square(n, f):
                pool.wait_ge(sq_ready, 8 * n + f + 1)
                if f == 0:
                    if n:
                        pool.wait_ge(rb_ready, n)
                    nc.gpsimd.tensor_copy(ACC[:], S[:, 0, :]).then_inc(sq_added, 1)
                else:
                    pool.wait_ge(sq_added, 8 * n + f)
                    TT(ACC[:], ACC[:], S[:, f % 2, :], ALU.add).then_inc(sq_added, 1)

            def rsqrt(n):
                pool.wait_ge(ms_ready, n + 1)
                pool.wait_ge(const_set, 2)
                TT(rtok, ms, half_neg, ALU.pow).then_inc(rtok_ready, 1)

            rsqrt(0)

            chain = [0]

            def link(ins):
                chain[0] += 1
                ins.then_inc(pchain, 1)
                pool.wait_ge(pchain, chain[0])

            TS = nc.gpsimd.tensor_scalar
            LR, LI, DT, ZR, MAG, PHI = (lam[:, n, :] for n in (0, 1, 3, 4, 5, 6))
            T1, T2, T3, RED, REDC, SN, CS = (lam[:, n, :] for n in (7, 8, 9, 10, 11, 12, 13))
            AR, AI = lam[:, 14, :], lam[:, 15, :]
            FR, FI, NRR, RHO, MINUS = (lam[:, n, :] for n in (16, 17, 18, 19, 20))
            link(nc.gpsimd.memset(MINUS, -1.0))
            pool.wait_ge(ssm_loaded, 16 * 17)
            pool.wait_ge(dt_ready, 1)
            TT(ZR, LR, DT, ALU.mult).then_inc(angle_ready, 1)
            link(TT(PHI, LI, DT, ALU.mult))
            TWO_PI = 2 * np.pi
            P1 = 6.28125
            P2 = float(np.float32(round((TWO_PI - P1) * 2 ** 20) / 2 ** 20))
            P3 = float(TWO_PI - P1 - P2)
            ROUND = 1.5 * 2 ** 23
            link(TS(T1, PHI, float(1 / TWO_PI), None, ALU.mult))
            link(TS(T1, T1, ROUND, None, ALU.add))
            link(TS(T1, T1, ROUND, None, ALU.subtract))
            link(TS(T2, T1, P1, None, ALU.mult))
            link(TT(PHI, PHI, T2, ALU.subtract))
            link(TS(T2, T1, P2, None, ALU.mult))
            link(TT(PHI, PHI, T2, ALU.subtract))
            link(TS(T2, T1, P3, None, ALU.mult))
            link(TT(PHI, PHI, T2, ALU.subtract))
            PI = float(np.nextafter(np.float32(np.pi), np.float32(0)))
            link(TS(RED, PHI, PI, -PI, ALU.min, ALU.max))
            link(TS(T1, RED, 0.0, None, ALU.max))
            link(TS(T3, RED, 0.0, None, ALU.min))
            link(TT(T3, T1, T3, ALU.subtract))
            TS(REDC, T3, -1.0, float(np.pi / 2), ALU.mult, ALU.add).then_inc(angle_ready, 2)
            pool.wait_ge(trig_ready, 3)

            def unit(cr, ci):
                link(TT(T1, cr, cr, ALU.mult))
                link(TT(T2, ci, ci, ALU.mult))
                link(TT(T1, T1, T2, ALU.add))
                link(TS(T1, T1, -0.5, 1.5, ALU.mult, ALU.add))
                link(TT(cr, cr, T1, ALU.mult))
                link(TT(ci, ci, T1, ALU.mult))
            unit(CS, SN)
            link(TT(AR, MAG, CS, ALU.mult))
            link(TT(AI, MAG, SN, ALU.mult))
            link(TS(NRR, AR, -1.0, None, ALU.add))
            link(TT(T1, LR, LR, ALU.mult))
            link(TT(T2, LI, LI, ALU.mult))
            link(TT(T1, T1, T2, ALU.add))
            link(TT(T3, T1, MINUS, ALU.pow))
            link(TT(T1, NRR, LR, ALU.mult))
            link(TT(T2, AI, LI, ALU.mult))
            link(TT(T1, T1, T2, ALU.add))
            link(TT(FR, T1, T3, ALU.mult))
            link(TT(T1, AI, LR, ALU.mult))
            link(TT(T2, NRR, LI, ALU.mult))
            link(TT(T1, T1, T2, ALU.subtract))
            link(TT(FI, T1, T3, ALU.mult))

            def cmul(dr, di, ar, ai, br, bi, t1, t2):
                link(TT(t1, ar, br, ALU.mult))
                link(TT(t2, ai, bi, ALU.mult))
                link(TT(t1, t1, t2, ALU.subtract))
                link(TT(t2, ar, bi, ALU.mult))
                link(TT(di, ai, br, ALU.mult))
                link(TT(di, di, t2, ALU.add))
                link(nc.gpsimd.tensor_copy(dr, t1))

            def over_c(a):
                return a.rearrange("p (a o) -> p a o", o=1).to_broadcast([P, PAIRS, C])
            pool.wait_ge(rb_ready, 1)
            c1_, c2_ = (ct[:, n, :].rearrange("p (a c) -> p a c", c=C) for n in (0, 1))
            cmul(Bbr[:], Bbi[:], Br[:], Bi[:], over_c(FR), over_c(FI), c1_, c2_)
            link(nc.gpsimd.memset(Ar[:, 0, :], 1.0))
            link(nc.gpsimd.memset(Ai[:, 0, :], 0.0))
            link(nc.gpsimd.tensor_copy(Ar[:, 1, :], AR))
            link(nc.gpsimd.tensor_copy(Ai[:, 1, :], AI))
            for n in range(2, TAU + 1):
                a, b = (n // 2, n - n // 2)
                cmul(Ar[:, n, :], Ai[:, n, :], Ar[:, a, :], Ai[:, a, :], Ar[:, b, :], Ai[:, b, :], T1, T2)
            link(TT(RHO, MAG, MAG, ALU.mult))
            link(TT(RHO, RHO, RHO, ALU.mult))
            link(TT(RHO, RHO, RHO, ALU.mult))
            for _n in range(3):
                cmul(CS, SN, CS, SN, CS, SN, T1, T2)
            unit(CS, SN)
            link(nc.gpsimd.memset(RC[:, :, 0:1], 1.0))
            link(nc.gpsimd.memset(RS[:, :, 0:1], 0.0))
            m = 1
            while m < CH:
                parts = max(1, PAIRS * m // 512)
                for h in range(parts):
                    n = PAIRS // parts
                    pr = slice(n * h, n * (h + 1))
                    t1, t2 = (rt[:, i, 0:n * m].rearrange("p (a m) -> p a m", m=m) for i in (0, 1))
                    wr, wi = (w[:, pr].rearrange("p (a o) -> p a o", o=1).to_broadcast([P, n, m]) for w in (CS, SN))
                    cmul(RC[:, pr, m:2 * m], RS[:, pr, m:2 * m], RC[:, pr, 0:m], RS[:, pr, 0:m], wr, wi, t1, t2)
                m *= 2
                if m < CH:
                    cmul(CS, SN, CS, SN, CS, SN, T1, T2)
                    unit(CS, SN)
            pool.wait_ge(c_ready, 16)
            pool.wait_ge(x_out, 16 * 8)
            pool.wait_ge(xl_ready, 8)
            for n in range(TAU + 1):
                ar, ai = over_c(Ar[:, n, :]), over_c(Ai[:, n, :])
                link(TT(c1_, Cr[:], ar, ALU.mult))
                link(TT(c2_, nCi[:], ai, ALU.mult))
                link(TT(FXr[:, :, n, :], c1_, c2_, ALU.add))
                link(TT(c1_, nCi[:], ar, ALU.mult))
                link(TT(c2_, Cr[:], ai, ALU.mult))
                link(TT(FXi[:, :, n, :], c1_, c2_, ALU.subtract))
            for src, dst in ((Bbr, BBr), (Bbi, BBi)):
                link(nc.gpsimd.memset(dst[:], 0.0))
                for g2 in range(2):
                    pp = slice(g2 * NS, (g2 + 1) * NS)
                    link(nc.gpsimd.tensor_copy(dst[pp, :, g2, :], src[pp]))
            pool.wait_ge(tile_done, START["glu"])
            for n in range(2):
                pool.wait_ge(u_out[n], 32)
            for t in range(TAU):
                n = TAU - 1 - t
                ar, ai = over_c(Ar[:, n, :]), over_c(Ai[:, n, :])
                link(TT(c1_, Bbr[:], ar, ALU.mult))
                link(TT(c2_, Bbi[:], ai, ALU.mult))
                link(TT(M1r[:, :, t, :], c1_, c2_, ALU.subtract))
                link(TT(c1_, Bbi[:], ar, ALU.mult))
                link(TT(c2_, Bbr[:], ai, ALU.mult))
                link(TT(M1i[:, :, t, :], c1_, c2_, ALU.add))
            nc.gpsimd.tensor_copy(lam[:, 21, :], RHO).then_inc(rot_ready, 1)
            nc.gpsimd.tensor_copy(lam[:, 22, :], RHO).then_inc(m1_ready, 1)
            pool.wait_ge(s_ready, 16)
            nc.gpsimd.memset(Lm[:], 0.0).then_inc(l_zero, 1)
            link(TT(kd[:], dsk[:].rearrange("p (a o) -> p a o", o=1).to_broadcast([32, PAIRS, C]),
                    eye16[:].rearrange("p (o c) -> p o c", o=1).to_broadcast([32, PAIRS, C]), ALU.mult))
            pool.wait_ge(kt_copied, 2)
            TT(Kt[:, :, 0:C], Kt[:, :, 0:C], kd[:], ALU.add).then_inc(k_copied, 1)
            rsqrt(1)

            for f in range(KD):
                add_square(2, f)
            pool.wait_ge(x_out, 16 * 16)
            pool.wait_ge(xl_ready, 16)
            nc.gpsimd.memset(F[:], 0.0).then_inc(f_zero, 1)
            rsqrt(2)
            rsqrt(3)
            for f in range(KD):
                add_square(4, f)
            rsqrt(4)
            pool.wait_ge(ws_c, 1)
            nc.gpsimd.affine_select(wst[:], wst[:], [[0, 8], [1, P]], ALU.is_ge, 0.0, base=0, channel_multiplier=-1
                                    ).then_inc(ws_m, 1)
            for t in range(MT):
                pool.wait_ge(ln_var, t + 1)
                TT(lnr, lnv, half_neg[:, 0:1], ALU.pow).then_inc(ln_r, 1)

            def merge2(stage, n):
                def turn(i):
                    for t in (2, 3):
                        ev_wait(pool, START[stage] + t, 4, i)
                        f = plus(t - 2, 2, i)
                        if n:
                            pool.wait_ge(m_added, plus(8 * (n - 1) + t - 1, 2, i))
                            TT(row(M, f), row(M, f), S[:, t % 2, :], ALU.add).then_inc(m_added, 1)
                        else:
                            nc.gpsimd.tensor_copy(row(M, f), S[:, t % 2, :]).then_inc(m_added, 1)
                repeat(pool, 4, turn)
            merge2("amerge", 0)
            merge2("bmerge", 1)
            merge2("cmerge", 2)
            for m in range(MT):
                pool.wait_ge(fv_r, m + 1)
                TT(fr[:, m:m + 1], fv[:, m:m + 1], half_neg[:, 0:1], ALU.pow).then_inc(fr_r, 1)


INPUTS = ["x", "norm_mix_pre", "norm_mix_post", "norm_mlp_pre", "norm_mlp_post", "w_in", "rel_bias", "sinks", "lam_re",
          "lam_im", "log_dt", "b_re", "b_im", "c_re", "c_im", "d_skip", "w_glu", "w_attn_branch", "w_ssm_branch",
          "w_out", "w_ff_in", "w_ff_out", "norm_g_2", "w_in_2", "ln_g_2", "ln_b_2", "w_s_2", "b_s_2", "conv_w_2",
          "conv_b_2", "w_pool_2", "pool_scale_2", "w_pa_2", "w_pb_2", "w_pc_2", "w_o_2", "final_g_2"]


def shape_constants():
    window = np.array([[w / min(t + 1, w) for t in range(16)] for w in POOLS], np.float32)
    return {"eye": np.eye(P, dtype=np.float32), "eye16": np.tile(np.eye(C, dtype=np.float32), (2, 1)),
            "bucket_rows": bucket_rows(), "window_scale": window}


def kernel(**inputs):
    import concourse.bacc as bacc
    from concourse.bass_utils import run_bass_kernel_spmd

    nc = bacc.Bacc("TRN2", target_bir_lowering=False, num_devices=1)
    arrays = {name: np.ascontiguousarray(inputs[name]) for name in INPUTS}
    arrays.update(shape_constants())
    io = {name: nc.dram_tensor(f"in_{name}", a.shape, mybir.dt.from_np(a.dtype), kind="ExternalInput").ap()
          for name, a in arrays.items()}
    out = nc.dram_tensor("out", (1, SEQ, D), mybir.dt.float32, kind="ExternalOutput").ap()
    hybrid_kernel(nc, io, out)
    r = run_bass_kernel_spmd(nc, [{f"in_{name}": a for name, a in arrays.items()}], core_ids=[0])
    return r.results[0]["out"]
```
